# Optimizing a Trainium2 kernel written in Bass

```python
import math
import jax, jax.numpy as jnp
from jax import lax
import numpy as np

D_MODEL = 2048
BATCH = 1
SEQ = 512
DEPTH = 1

RNN_WIDTH = D_MODEL // 2
RNN_BLOCKS = 16
RNN_BLOCK_DIM = RNN_WIDTH // RNN_BLOCKS
CONV_WIDTH = 4
LRU_C = 8.0
N_HEADS = 8
HEAD_DIM = 128
ATTN_WIDTH = N_HEADS * HEAD_DIM
IDX_HEADS = 16
IDX_DIM = 64
INDEX_TOPK_MAX = 256
Q_BLOCK = 64
D_FF = 4 * D_MODEL
NORM_EPS = 1e-6
SPLITS = (RNN_WIDTH, RNN_WIDTH, ATTN_WIDTH, ATTN_WIDTH, ATTN_WIDTH,
          IDX_HEADS * IDX_DIM, IDX_DIM, IDX_HEADS, D_MODEL, D_MODEL)
D_IN = sum(SPLITS)
SPLIT_OFFSETS = tuple(int(o) for o in np.cumsum(SPLITS)[:-1])

kernel_name = 'hybrid_rglru_dsa_gated_block'

def rms_norm(x, g):
    xf = x.astype(jnp.float32)
    y = xf * lax.rsqrt(jnp.mean(xf * xf, axis=-1, keepdims=True) + NORM_EPS)
    return (y * g.astype(jnp.float32)).astype(x.dtype)

def causal_depthwise_conv(x, w, b):
    S = x.shape[1]
    xp = jnp.pad(x, ((0, 0), (CONV_WIDTH - 1, 0), (0, 0)))
    y = b
    for j in range(CONV_WIDTH):
        y = y + w[j] * xp[:, j:j + S]
    return y

def block_diag_linear(x, w, b):
    B, S, C = x.shape
    xb = x.reshape(B, S, RNN_BLOCKS, RNN_BLOCK_DIM)
    y = jnp.einsum('bsnd,nde->bsne', xb, w).reshape(B, S, C)
    return y + b

def rg_lru(x, w_r, b_r, w_i, b_i, lam):
    xf = x.astype(jnp.float32)
    r = jax.nn.sigmoid(block_diag_linear(xf, w_r.astype(jnp.float32), b_r.astype(jnp.float32)))
    i = jax.nn.sigmoid(block_diag_linear(xf, w_i.astype(jnp.float32), b_i.astype(jnp.float32)))
    log_a = -LRU_C * r * jax.nn.softplus(-lam.astype(jnp.float32))
    a = jnp.exp(log_a)
    mult = jnp.sqrt(-jnp.expm1(2.0 * log_a))
    u = mult * i * xf

    def combine(left, right):
        a1, b1 = left
        a2, b2 = right
        return a1 * a2, a2 * b1 + b2

    _, h = lax.associative_scan(combine, (a, u), axis=1)
    return h.astype(x.dtype)

def dsa_sparse_attention(q, k, v, iq, ik, iw, slopes):
    B, S = q.shape[0], q.shape[1]
    n_keys = S
    topk = min(INDEX_TOPK_MAX, n_keys // 4)
    n_blocks = S // Q_BLOCK
    key_pos = jnp.arange(S, dtype=jnp.int32)
    idx_scale = IDX_DIM ** -0.5
    w_scale = IDX_HEADS ** -0.5
    attn_scale = HEAD_DIM ** -0.5

    def one_block(blk):
        start = blk * Q_BLOCK
        qb = lax.dynamic_slice_in_dim(q, start, Q_BLOCK, axis=1)
        iqb = lax.dynamic_slice_in_dim(iq, start, Q_BLOCK, axis=1)
        iwb = lax.dynamic_slice_in_dim(iw, start, Q_BLOCK, axis=1)
        q_pos = start + jnp.arange(Q_BLOCK, dtype=jnp.int32)
        logits = jnp.einsum('bqhd,bsd->bqhs', iqb, ik).astype(jnp.float32) * idx_scale
        index_score = jnp.einsum('bqhs,bqh->bqs', jax.nn.relu(logits),
                                 iwb.astype(jnp.float32) * w_scale)
        causal = key_pos[None, :] <= q_pos[:, None]
        index_score = jnp.where(causal[None], index_score, -jnp.inf)
        _, sel = lax.top_k(index_score, topk)
        k_sel = jax.vmap(lambda kk, ii: kk[ii])(k, sel)
        v_sel = jax.vmap(lambda vv, ii: vv[ii])(v, sel)
        s = jnp.einsum('bqhd,bqkhd->bhqk', qb, k_sel).astype(jnp.float32) * attn_scale
        dist = (q_pos[None, :, None] - sel).astype(jnp.float32)
        s = s - slopes[None, :, None, None] * dist[:, None]
        valid = sel <= q_pos[None, :, None]
        s = jnp.where(valid[:, None], s, -jnp.inf)
        p = jax.nn.softmax(s, axis=-1).astype(v.dtype)
        o = jnp.einsum('bhqk,bqkhd->bqhd', p, v_sel)
        return o.reshape(B, Q_BLOCK, N_HEADS * HEAD_DIM)

    out = lax.map(one_block, jnp.arange(n_blocks, dtype=jnp.int32))
    return out.transpose(1, 0, 2, 3).reshape(B, S, N_HEADS * HEAD_DIM)

def setup_inputs(seed: int = 0) -> dict:
    key = jax.random.key(seed)
    ks = jax.random.split(key, 20)
    f32 = jnp.float32

    def nrm(k, shape, fan_in):
        return jax.random.normal(k, shape, f32) * (fan_in ** -0.5)

    x = jax.random.normal(ks[0], (BATCH, SEQ, D_MODEL), f32)
    norm_mix_g = 1.0 + 0.02 * jax.random.normal(ks[1], (DEPTH, D_MODEL), f32)
    w_in = nrm(ks[2], (DEPTH, D_MODEL, D_IN), D_MODEL)
    conv_w = nrm(ks[3], (DEPTH, CONV_WIDTH, RNN_WIDTH), CONV_WIDTH)
    conv_b = 0.02 * jax.random.normal(ks[4], (DEPTH, RNN_WIDTH), f32)
    w_rg_r = nrm(ks[5], (DEPTH, RNN_BLOCKS, RNN_BLOCK_DIM, RNN_BLOCK_DIM), RNN_BLOCK_DIM)
    b_rg_r = 0.02 * jax.random.normal(ks[6], (DEPTH, RNN_WIDTH), f32)
    w_rg_i = nrm(ks[7], (DEPTH, RNN_BLOCKS, RNN_BLOCK_DIM, RNN_BLOCK_DIM), RNN_BLOCK_DIM)
    b_rg_i = 0.02 * jax.random.normal(ks[8], (DEPTH, RNN_WIDTH), f32)
    u = jax.random.uniform(ks[9], (DEPTH, RNN_WIDTH), f32, 0.9, 0.999)
    a0 = u ** (1.0 / LRU_C)
    lru_lambda = jnp.log(a0) - jnp.log1p(-a0)
    w_branch_rnn = nrm(ks[10], (DEPTH, RNN_WIDTH, D_MODEL), RNN_WIDTH)
    w_branch_attn = nrm(ks[11], (DEPTH, ATTN_WIDTH, D_MODEL), ATTN_WIDTH)
    w_out = nrm(ks[12], (DEPTH, D_MODEL, D_MODEL), D_MODEL)
    norm_mlp_g = 1.0 + 0.02 * jax.random.normal(ks[13], (DEPTH, D_MODEL), f32)
    w_mlp_up = nrm(ks[14], (DEPTH, D_MODEL, D_FF), D_MODEL)
    w_mlp_down = nrm(ks[15], (DEPTH, D_FF, D_MODEL), D_FF)
    norm_final_g = 1.0 + 0.02 * jax.random.normal(ks[16], (D_MODEL,), f32)
    return {'x': x, 'norm_mix_g': norm_mix_g, 'w_in': w_in, 'conv_w': conv_w,
            'conv_b': conv_b, 'w_rg_r': w_rg_r, 'b_rg_r': b_rg_r, 'w_rg_i': w_rg_i,
            'b_rg_i': b_rg_i, 'lru_lambda': lru_lambda, 'w_branch_rnn': w_branch_rnn,
            'w_branch_attn': w_branch_attn, 'w_out': w_out, 'norm_mlp_g': norm_mlp_g,
            'w_mlp_up': w_mlp_up, 'w_mlp_down': w_mlp_down, 'norm_final_g': norm_final_g}

def reference(x, norm_mix_g, w_in, conv_w, conv_b, w_rg_r, b_rg_r, w_rg_i, b_rg_i,
              lru_lambda, w_branch_rnn, w_branch_attn, w_out, norm_mlp_g,
              w_mlp_up, w_mlp_down, norm_final_g):
    B, S, _ = x.shape
    slopes = 2.0 ** (-8.0 * jnp.arange(1, N_HEADS + 1, dtype=jnp.float32) / N_HEADS)
    h = x
    for l in range(DEPTH):
        u = rms_norm(h, norm_mix_g[l])
        proj = u @ w_in[l]
        (rx, rgate, q, k, v, iq, ik, iw, gate_a, gate_b) = jnp.split(proj, SPLIT_OFFSETS, axis=-1)
        xc = causal_depthwise_conv(rx, conv_w[l], conv_b[l])
        ya = rg_lru(xc, w_rg_r[l], b_rg_r[l], w_rg_i[l], b_rg_i[l], lru_lambda[l]) * jax.nn.gelu(rgate)
        yb = dsa_sparse_attention(q.reshape(B, S, N_HEADS, HEAD_DIM),
                                  k.reshape(B, S, N_HEADS, HEAD_DIM),
                                  v.reshape(B, S, N_HEADS, HEAD_DIM),
                                  iq.reshape(B, S, IDX_HEADS, IDX_DIM), ik, iw, slopes)
        mixed = (jax.nn.sigmoid(gate_a) * (ya @ w_branch_rnn[l])
                 + jax.nn.sigmoid(gate_b) * (yb @ w_branch_attn[l]))
        h = h + mixed @ w_out[l]
        u = rms_norm(h, norm_mlp_g[l])
        h = h + jnp.square(jax.nn.relu(u @ w_mlp_up[l])) @ w_mlp_down[l]
    return rms_norm(h, norm_final_g)


_drawn_inputs = setup_inputs


def setup_inputs(seed=0):
    import zlib

    import numpy as np

    out = dict(_drawn_inputs(seed))
    spreads = {}
    factors = {'b_rg_r': 48.384, 'b_rg_i': 36.994, 'norm_mlp_g': 3.154, 'norm_final_g': 8.465}
    for name, (base, spread) in spreads.items():
        noise = np.random.default_rng([zlib.crc32(name.encode()), seed]).standard_normal(out[name].shape)
        drawn = base * np.exp(spread * noise) if base else spread * noise
        out[name] = __import__('jax').numpy.asarray(drawn.astype(out[name].dtype))
    for name, factor in factors.items():
        out[name] = (out[name] * factor).astype(out[name].dtype)
    return out
```

```python
import numpy as np

import concourse.bass as bass
from concourse import mybir

F32 = mybir.dt.float32
F32R = mybir.dt.float32r
ACT = mybir.ActivationFunctionType
ALU = mybir.AluOpType
AX = mybir.AxisListType

P = 128
S = 512
D = 2048
RNN = D // 2
HEADS = 8
HD = 128
IDX_HEADS = 16
IDX_DIM = 64
D_FF = 4 * D
TOPK = min(256, S // 4)
LRU_C = 8.0
EPS = 1e-6
TT = S // P
KD = D // P
KR = RNN // P
PAD = 4
RXW = S + PAD

C_RX, C_RG, C_Q, C_K, C_V = 0, RNN, 2 * RNN, 3 * RNN, 4 * RNN
C_IQ = 5 * RNN
C_IK = C_IQ + IDX_HEADS * IDX_DIM
C_GA = C_IK + IDX_DIM + IDX_HEADS
C_GB = C_GA + D
IKW = IDX_DIM + IDX_HEADS

U_IQRX = 1
U_RG = U_IQRX + 16
U_GA = U_RG + 8
U_WR = U_GA + 16
U_HD = U_WR + 8
U_GB = U_HD + 24
U_WO = U_GB + 24
U_ML = U_WO + 16
MLP_GROUPS = 8
UNITS = U_ML + MLP_GROUPS * 16
B_IQRX = 1
B_RG = B_IQRX + 16
B_GA = B_RG + 8
B_WR = B_GA + 16
B_HD = B_WR + 16
B_GB = B_HD + 24
B_WO = B_GB + 32
B_ML = B_WO + 16

NEG = -3.0e38
CHUNK_W = [P * (t + 1) for t in range(TT)]
CHUNK_O = [sum(CHUNK_W[:t]) for t in range(TT)]
PACKED = sum(CHUNK_W)

PR_GMIX, PR_GMLP, PR_CW, PR_CB, PR_BR, PR_BI, PR_LAM = 0, 16, 32, 64, 72, 80, 88
PR_ROWS = 96

LRU_DVE = ["conv0", "conv1", "conv2", "conv3", "asq", "var", "gated", "u", "scan", "y", "lo"]
LRU_ACT = ["r", "i", "a", "th", "mult", "hi"]


def lru_dve(i, step, j):
    return 2 * len(LRU_DVE) * i + 2 * LRU_DVE.index(step) + j + 1


def lru_act(i, step, j):
    return 2 * len(LRU_ACT) * i + 2 * LRU_ACT.index(step) + j + 1


class Semaphores:

    def __init__(self, nc):
        self.x_in = nc.alloc_semaphore("x_in")
        self.par_in = nc.alloc_semaphore("par_in")
        self.g_in = nc.alloc_semaphore("g_in")
        self.ikd_in = nc.alloc_semaphore("ikd_in")
        self.bd_in = nc.alloc_semaphore("bd_in")
        self.h_in = nc.alloc_semaphore("h_in")
        self.out_st = nc.alloc_semaphore("out_st")
        self.ident_ok = nc.alloc_semaphore("ident_ok")
        self.zeros_ok = nc.alloc_semaphore("zeros_ok")
        self.mask_ok = nc.alloc_semaphore("mask_ok")
        self.par_t = nc.alloc_semaphore("par_t")
        self.par_ok = nc.alloc_semaphore("par_ok")
        self.lam_step = nc.alloc_semaphore("lam_step")
        self.x_ready = nc.alloc_semaphore("x_ready")
        self.xs_ready = nc.alloc_semaphore("xs_ready")
        self.ss_ready = nc.alloc_semaphore("ss_ready")
        self.rs_ready = nc.alloc_semaphore("rs_ready")
        self.feat_t = nc.alloc_semaphore("feat_t")
        self.feat_hi = nc.alloc_semaphore("feat_hi")
        self.feat_lo = nc.alloc_semaphore("feat_lo")
        self.hi_ready = nc.alloc_semaphore("hi_ready")
        self.lo_ready = nc.alloc_semaphore("lo_ready")
        self.quarter = nc.alloc_semaphore("quarter")
        self.drained = nc.alloc_semaphore("drained")
        self.iwt = nc.alloc_semaphore("iwt")
        self.iw_ok = nc.alloc_semaphore("iw_ok")
        self.idx_mm = nc.alloc_semaphore("idx_mm")
        self.relu_done = nc.alloc_semaphore("relu_done")
        self.acc_done = nc.alloc_semaphore("acc_done")
        self.topk_step = nc.alloc_semaphore("topk_step")
        self.sel_ok = nc.alloc_semaphore("sel_ok")
        self.lru_mm = nc.alloc_semaphore("lru_mm")
        self.lru_v = nc.alloc_semaphore("lru_v")
        self.lru_a = nc.alloc_semaphore("lru_a")
        self.scores_ready = nc.alloc_semaphore("scores_ready")
        self.biased = nc.alloc_semaphore("biased")
        self.negmax = nc.alloc_semaphore("negmax")
        self.exped = nc.alloc_semaphore("exped")
        self.recip = nc.alloc_semaphore("recip")
        self.normed = nc.alloc_semaphore("normed")
        self.p_t = nc.alloc_semaphore("p_t")
        self.pt_done = nc.alloc_semaphore("pt_done")
        self.v_t = nc.alloc_semaphore("v_t")
        self.vt_ok = nc.alloc_semaphore("vt_ok")
        self.av_ready = nc.alloc_semaphore("av_ready")
        self.yb_done = nc.alloc_semaphore("yb_done")
        self.yb_hi = nc.alloc_semaphore("yb_hi")
        self.yb_lo = nc.alloc_semaphore("yb_lo")
        self.mix_ok = nc.alloc_semaphore("mix_ok")
        self.mix_hi = nc.alloc_semaphore("mix_hi")
        self.mix_lo = nc.alloc_semaphore("mix_lo")
        self.ss2_ok = nc.alloc_semaphore("ss2_ok")
        self.rs2_ok = nc.alloc_semaphore("rs2_ok")
        self.mlp_hi = nc.alloc_semaphore("mlp_hi")
        self.mlp_sq = nc.alloc_semaphore("mlp_sq")
        self.mlp_lo = nc.alloc_semaphore("mlp_lo")
        self.fin_ss = nc.alloc_semaphore("fin_ss")
        self.fin_rs = nc.alloc_semaphore("fin_rs")
        self.fin_ok = nc.alloc_semaphore("fin_ok")
        self.raw_in = [nc.alloc_semaphore(f"raw_in{k}") for k in range(2)]


def hybrid_block(nc, x, g_mix, w_in, conv_w, conv_b, w_r, b_r, w_i, b_i, lam, w_br, w_ba, w_out,
                 g_mlp, w_up, w_down, g_fin, out):
    KB = 1024
    BASE = (nc.sbuf_base + 63) // 64 * 64

    def at(name, kb, shape, dt):
        return nc.alloc_sbuf_tensor_at(name, shape, dt, offset=BASE + int(kb * KB))

    raw = [at(f"raw{s}", 8 * s, [P, 2048], F32) for s in range(2)]
    whi = [at(f"whi{s}", 16 + 8 * s, [P, 2048], F32R) for s in range(2)]
    wlo = [at(f"wlo{s}", 32 + 8 * s, [P, 2048], F32R) for s in range(2)]
    uhi = at("uhi", 48, [P, KD, S], F32R)
    ulo = at("ulo", 80, [P, KD, S], F32R)
    mhi = at("mhi", 48, [P, KD, S], F32R)
    mlo = at("mlo", 80, [P, KD, S], F32R)
    vhi = at("vhi", 48, [P, KD, S], F32R)
    vlo = at("vlo", 80, [P, KD, S], F32R)
    R3, R4 = 112, 144
    xt = at("xt", R3, [P, TT, D], F32)
    iq = at("iq", R3, [P, 4, S], F32)
    ikw = at("ikw", R3 + 8, [P, S], F32)
    ikd = at("ikd", R3 + 10, [P, S], F32)
    rbuf = at("rbuf", R3 + 12, [P, 4, S], F32)
    score = at("score", R3 + 20, [P, PACKED - P], F32)
    work = at("work", R3 + 24.5, [P, PACKED - P], F32)
    dist = at("dist", R3 + 29, [P, S], F32)
    mix = at("mix", R3, [P, KD, S], F32)
    hidhi = at("hidhi", R3, [P, 8, S], F32R)
    hidlo = at("hidlo", R3 + 16, [P, 8, S], F32R)

    junk1 = at("junk1", R4, [P, D], F32)
    rx = at("rx", R4, [P, KR, RXW], F32)
    yahi = at("yahi", R4, [P, KR, RXW], F32R)
    rg = at("rg", R4 + 16.125, [P, KR, S], F32)
    yalo = at("yalo", R4 + 16.125, [P, KR, S], F32R)
    lru = {n: at(f"lru_{n}", R4 + 32.125 + 4 * k, [P, 2, S], F32)
           for k, n in enumerate(["xc", "rr", "ii", "aa", "th"])}
    yb = at("yb", R4, [P, KR, S], F32)
    kf = at("kf", R4 + 16, [P, 2, S], F32)
    qf = at("qf", R4 + 20, [P, 2, S], F32)
    vf = at("vf", R4 + 24, [P, 2, S], F32)
    vt = at("vt", R4 + 28, [P, 2, TT, HD], F32)
    sm = at("sm", R4 + 32, [P, 2, PACKED], F32)
    pt = at("pt", R4 + 42, [P, PACKED], F32)
    ybhi = at("ybhi", R4 + 16, [P, KR, S], F32R)
    yblo = at("yblo", R4 + 32, [P, KR, S], F32R)
    gb = at("gb", R4 + 48, [P, 4, S], F32)
    h = at("h", R4, [P, TT, D], F32)
    relu_h = at("relu_h", R4 + 32, [P, 4, S], F32)
    sq_h = at("sq_h", R4 + 40, [P, 4, S], F32)
    junk2 = at("junk2", R4 + 48, [P, D], F32)
    finjunk = at("finjunk", R4 + 32, [P, D], F32)
    gfin = at("gfin", R4 + 48, [P, D], F32)
    ga_tmp = at("ga_tmp", R4 + 56, [P, 2, S], F32)

    top = 204.0
    ident = at("ident", top, [P, P], F32)
    par = at("par", top + 0.5, [P, PR_ROWS], F32)
    par_rows = at("par_rows", top + 0.875, [PR_ROWS, P], F32)
    bd = at("bd", top - 2.0, [P, 2, 2, P], F32)
    iwq = at("iwq", top + 1.375, [P, TT - 1, IDX_HEADS], F32)
    small = at("small", top + 1.5625, [P, 128], F32)
    sp_t = at("sp_t", top + 2.0625, [P, 8, 8], F32)
    slopes = at("slopes", top + 2.3125, [P, HEADS], F32)
    abias = at("abias", top - 7.0, [P, PACKED], F32)
    smneg, smsum, sminv = (small[:, 8 * k:8 * k + 8] for k in range(3))
    top8 = small[:, 24:32]
    ss1, rs1, ss2, rs2, ss3, rs3 = (small[:, 32 + 4 * k:36 + 4 * k] for k in range(6))
    eps = small[:, 64:65]
    sp8, nsp8 = sp_t[:, 6], sp_t[:, 7]

    stream = [nc.alloc_psum_tensor(f"stream{b}", [P, S], F32) for b in range(4)]
    aux = [nc.alloc_psum_tensor(f"aux{b}", [P, S], F32) for b in range(4)]
    bank = stream + aux

    s = Semaphores(nc)
    raw_in = s.raw_in

    w_in_k = w_in[0].rearrange("(k p) n -> p k n", p=P)
    w_br_k = w_br[0].rearrange("(k p) n -> p k n", p=P)
    w_ba_k = w_ba[0].rearrange("(k p) n -> p k n", p=P)
    w_out_k = w_out[0].rearrange("(k p) n -> p k n", p=P)
    w_up_k = w_up[0].rearrange("(k p) n -> p k n", p=P)
    w_down_k = w_down[0].rearrange("(k p) n -> p k n", p=P)
    x_t = x[0].rearrange("(t p) d -> p t d", p=P)
    out_t = out[0].rearrange("(t p) d -> p t d", p=P)

    def four(t):
        return t[:].rearrange("p (k n) -> p k n", k=4)

    def eight(t):
        return t[:].rearrange("p (k n) -> p k n", k=8)

    block = nc.Block()
    block.__enter__()

    @block.sync
    def _(sp):
        def load(n, slot, dst, src):
            if not isinstance(n, int) or n >= 2:
                sp.wait_ge(s.lo_ready, n - 1)
            sp.dma_start(dst, src).then_inc(raw_in[slot], 16)

        def blocks(n, cols, src, k0=0, units=4):
            for j in range(units):
                load(n + j, (U_IQRX + j) % 2, four(raw[(U_IQRX + j) % 2]),
                     src[:, k0 + 4 * j:k0 + 4 * j + 4, cols])

        load(0, 0, raw[0][:, 0:KD * IKW].rearrange("p (k n) -> p k n", k=KD),
             w_in_k[:, :, C_IK:C_IK + IKW])
        for i in range(2):
            blocks(U_IQRX + 8 * i, bass.ds(C_IQ + 512 * i, 512), w_in_k)
            blocks(U_IQRX + 8 * i + 4, bass.ds(C_RX + 512 * i, 512), w_in_k)
        with sp.Fori(0, 2) as i:
            blocks(U_RG + 4 * i, bass.ds(C_RG + 512 * i, 512), w_in_k)
        with sp.Fori(0, 4) as i:
            blocks(U_GA + 4 * i, bass.ds(C_GA + 512 * i, 512), w_in_k)
        with sp.Fori(0, 4) as i:
            blocks(U_WR + 2 * i, bass.ds(512 * i, 512), w_br_k, units=2)
        with sp.Fori(0, 4) as p:
            for j, c in enumerate((C_K, C_K, C_Q, C_Q, C_V, C_V)):
                slot = (U_HD + j) % 2
                load(U_HD + 6 * p + j, slot, eight(raw[slot]),
                     w_in_k[:, 8 * (j % 2):8 * (j % 2) + 8, bass.ds(c + 256 * p, 256)])
        with sp.Fori(0, 4) as i:
            blocks(U_GB + 6 * i, bass.ds(C_GB + 512 * i, 512), w_in_k)
            blocks(U_GB + 6 * i + 4, bass.ds(256 * (2 * i), 512), w_ba_k, units=2)
        with sp.Fori(0, 4) as i:
            blocks(U_WO + 4 * i, bass.ds(512 * i, 512), w_out_k)
        with sp.Fori(0, MLP_GROUPS) as g:
            for b in range(2):
                blocks(U_ML + 16 * g + 4 * b, bass.ds(1024 * g + 512 * b, 512), w_up_k)
            for c in range(4):
                for kh in range(2):
                    j = 8 + 2 * c + kh
                    slot = (U_ML + j) % 2
                    load(U_ML + 16 * g + j, slot, four(raw[slot]),
                         w_down_k[:, bass.ds(8 * g + 4 * kh, 4), 512 * c:512 * c + 512])

    @block.gpsimd
    def _(pool):
        pool.memset(ident[:], 0.0).then_inc(s.zeros_ok, 1)
        pool.memset(bd[:], 0.0).then_inc(s.zeros_ok, 1)
        pool.memset(eps, EPS).then_inc(s.zeros_ok, 1)
        for hh in range(HEADS):
            pool.memset(slopes[:, hh:hh + 1], 2.0 ** (-8.0 * (hh + 1) / HEADS)).then_inc(s.zeros_ok, 1)
        pool.wait_ge(s.zeros_ok, 3)
        pool.affine_select(out=ident[:], in_=ident[:], compare_op=ALU.not_equal, fill=1.0, base=0,
                           pattern=[[-1, P]], channel_multiplier=1).then_inc(s.ident_ok, 1)

        def load_bd(i):
            for j in range(2):
                for g, w in enumerate((w_r, w_i)):
                    for b in range(2):
                        pool.dma_start(bd[64 * b:64 * b + 64, j, g, 64 * b:64 * b + 64],
                                       w[0, bass.ds(4 * i + 2 * j + b, 1)].rearrange("a d e -> (a d) e")
                                       ).then_inc(s.bd_in, 16)
        load_bd(0)
        pool.wait_ge(s.feat_lo, KD)
        pool.iota(dist[:], [[1, S]], base=0, channel_multiplier=-1,
                  allow_small_or_imprecise_dtypes=True).then_inc(s.mask_ok, 1)
        pool.memset(score[:], 0.0).then_inc(s.mask_ok, 1)
        pool.memset(rx[:, :, 0:PAD], 0.0).then_inc(s.mask_ok, 1)
        pool.wait_ge(s.mask_ok, 3)
        for t in range(1, TT):
            o = CHUNK_O[t] - P
            v = score[:, o:o + CHUNK_W[t]]
            pool.affine_select(out=v, in_=v, compare_op=ALU.is_ge, fill=NEG, base=P * t,
                               pattern=[[-1, CHUNK_W[t]]], channel_multiplier=1).then_inc(s.mask_ok, 1)
        pool.affine_select(out=abias[:, 0:P], in_=dist[:, 0:P], compare_op=ALU.is_ge, fill=NEG, base=0,
                           pattern=[[-1, P]], channel_multiplier=1).then_inc(s.mask_ok, 1)
        with pool.Fori(1, 4) as i:
            pool.wait_ge(s.lru_mm, 2 * i)
            load_bd(i)
        pool.wait_ge(s.quarter, 4 * U_WO)
        pool.wait_ge(s.mix_ok, 16)
        pool.dma_start(h[:], x_t).then_inc(s.h_in, 16)
        pool.wait_ge(s.ss2_ok, TT)
        pool.dma_start(gfin[:], g_fin.rearrange("(a d) -> a d", a=1).broadcast_to([P, D])).then_inc(s.g_in, 16)

    @block.scalar
    def _(act):
        for t in range(TT):
            act.dma_start(xt[:, t], x_t[:, t]).then_inc(s.x_in, 16)
        for row, src, n in ((PR_GMIX, g_mix[0], 16), (PR_GMLP, g_mlp[0], 16), (PR_CB, conv_b[0], 8),
                            (PR_BR, b_r[0], 8), (PR_BI, b_i[0], 8), (PR_LAM, lam[0], 8)):
            act.dma_start(par_rows[row:row + n, :], src.rearrange("(c p) -> c p", p=P)).then_inc(s.par_in, 16)
        act.dma_start(par_rows[PR_CW:PR_CW + 32, :],
                      conv_w[0].rearrange("j (c p) -> (j c) p", p=P)).then_inc(s.par_in, 16)

        def hi(n, slot, landed, width=2048):
            act.wait_ge(raw_in[slot], 16 * landed)
            if not isinstance(n, int) or n >= 2:
                act.wait_ge(s.quarter, 4 * n - 4)
            nc.scalar.copy(whi[slot][:, 0:width], raw[slot][:, 0:width]).then_inc(s.hi_ready, 1)

        def next_hi(base, per, i, j):
            b = base + j + 1
            hi(b + per * i, b % 2, b // 2 + 1 + (per // 2) * i)

        act.wait_ge(s.zeros_ok, 3)
        for t in range(TT):
            act.wait_ge(s.x_in, 16 * TT)
            nc.scalar.activation(junk1[:], xt[:, t], ACT.Square, accum_out=ss1[:, t:t + 1]).then_inc(s.ss_ready, 1)
            act.wait_ge(s.ss_ready, t + 1)
            nc.scalar.activation(ss1[:, t:t + 1], ss1[:, t:t + 1], ACT.Sqrt, bias=eps, scale=1.0 / D).then_inc(s.rs_ready, 1)
        hi(0, 0, 1, KD * IKW)
        act.wait_ge(s.par_t, 1)
        nc.scalar.copy(par[:], bank[3][:, 0:PR_ROWS]).then_inc(s.par_ok, 1)
        act.wait_ge(s.par_ok, 1)
        act.wait_ge(s.lam_step, 2)
        nc.scalar.activation(sp_t[:, 1], sp_t[:, 0], ACT.Exp, scale=-1.0).then_inc(s.lam_step, 1)
        for c in range(KD):
            act.wait_ge(s.feat_t, c + 1)
            nc.scalar.activation(uhi[:, c], aux[c % 4][:], ACT.Copy, scale=par[:, PR_GMIX + c:PR_GMIX + c + 1]).then_inc(s.feat_hi, 1)
        hi(1, 1, 1)
        act.wait_ge(s.quarter, 4)
        act.wait_ge(s.feat_lo, KD)
        nc.scalar.copy(ikw[0:IKW, :], stream[0][0:IKW, :]).then_inc(s.drained, 1)
        act.wait_ge(s.drained, 1)
        act.dma_start(ikd[IDX_DIM:2 * IDX_DIM, :], ikw[0:IDX_DIM, :]).then_inc(s.ikd_in, 16)
        act.wait_ge(s.iwt, 1)
        nc.scalar.activation(iwq[:], aux[0][:, 0:(TT - 1) * IKW].rearrange("p (t c) -> p t c", t=TT - 1)[:, :, IDX_DIM:IKW],
                             ACT.Copy, scale=IDX_DIM ** -0.5 * IDX_HEADS ** -0.5).then_inc(s.iw_ok, 1)
        act.sem_inc(s.relu_done, 4)

        def relu_step(i, st):
            t = 1 + st % 3
            for hh in range(2):
                b = 2 * (st % 2) + hh
                act.wait_ge(s.acc_done, 24 * i + 2 * st + hh + 1)
                act.wait_ge(s.idx_mm, 24 * i + 2 * st + hh + 1)
                nc.scalar.activation(rbuf[:, b, 0:CHUNK_W[t]], aux[b][:, 0:CHUNK_W[t]], ACT.Relu).then_inc(s.relu_done, 1)

        with act.Fori(0, 2) as i:
            for j in range(8):
                next_hi(U_IQRX, 8, i, j)
                for q in range(4):
                    if j == 3:
                        act.wait_ge(s.quarter, 4 * (U_IQRX + 3) + q + 1 + 32 * i)
                        nc.scalar.copy(iq[:, q], stream[q][:]).then_inc(s.drained, 1)
                    if j == 7:
                        act.wait_ge(s.quarter, 4 * (U_IQRX + 7) + q + 1 + 32 * i)
                        nc.scalar.copy(rx[:, bass.ds(4 * i + q, 1), PAD:RXW].rearrange("p a n -> p (a n)"), stream[q][:]).then_inc(s.drained, 1)
                    if j >= 4 and q < 3:
                        relu_step(i, 3 * (j - 4) + q)
        with act.Fori(0, 2) as i:
            for j in range(4):
                next_hi(U_RG, 4, i, j)
            for q in range(4):
                act.wait_ge(s.quarter, 4 * (U_RG + 3) + q + 1 + 16 * i)
                nc.scalar.activation(rg[:, bass.ds(4 * i + q, 1)].rearrange("p a n -> p (a n)"), stream[q][:], ACT.Gelu_apprx_tanh).then_inc(s.drained, 1)
        act.wait_ge(s.lam_step, 23)
        act.wait_ge(s.sel_ok, 3)
        with act.Fori(0, 4) as i:
            next_hi(U_GA, 4, i, 0)
            next_hi(U_GA, 4, i, 1)
            for j in range(2):
                act.wait_ge(s.lru_mm, 2 * i + j + 1)
                nc.scalar.activation(lru["rr"][:, j], aux[2 * j][:], ACT.Sigmoid, bias=par[:, bass.ds(PR_BR + 2 * i + j, 1)]).then_inc(s.lru_a, 1)
            for j in range(2):
                nc.scalar.activation(lru["ii"][:, j], aux[2 * j + 1][:], ACT.Sigmoid, bias=par[:, bass.ds(PR_BI + 2 * i + j, 1)]).then_inc(s.lru_a, 1)
            for j in range(2):
                act.wait_ge(s.lru_a, lru_act(i, "r", j))
                nc.scalar.activation(lru["aa"][:, j], lru["rr"][:, j], ACT.Exp, scale=nsp8[:, bass.ds(2 * i + j, 1)]).then_inc(s.lru_a, 1)
            for j in range(2):
                nc.scalar.activation(lru["th"][:, j], lru["rr"][:, j], ACT.Tanh, scale=sp8[:, bass.ds(2 * i + j, 1)]).then_inc(s.lru_a, 1)
            next_hi(U_GA, 4, i, 2)
            for j in range(2):
                act.wait_ge(s.lru_v, lru_dve(i, "var", j))
                nc.scalar.activation(lru["rr"][:, j], lru["th"][:, j], ACT.Sqrt).then_inc(s.lru_a, 1)
            for j in range(2):
                act.wait_ge(s.lru_v, lru_dve(i, "y", j))
                nc.scalar.copy(yahi[:, bass.ds(2 * i + j, 1), 0:S].rearrange("p a n -> p (a n)"), lru["xc"][:, j]).then_inc(s.lru_a, 1)
            next_hi(U_GA, 4, i, 3)
            for q in range(4):
                act.wait_ge(s.quarter, 4 * (U_GA + 3) + q + 1 + 16 * i)
                nc.scalar.activation(mix[:, bass.ds(4 * i + q, 1)].rearrange("p a n -> p (a n)"), stream[q][:], ACT.Sigmoid).then_inc(s.drained, 1)
        with act.Fori(0, 4) as i:
            next_hi(U_WR, 2, i, 0)
            next_hi(U_WR, 2, i, 1)

        def exp_of(H, j):
            act.wait_ge(s.negmax, 4 * H + 4)
            for t in range(TT):
                o = CHUNK_O[t]
                v = sm[:, j, o:o + CHUNK_W[t]]
                nc.scalar.activation(v, v, ACT.Exp, bias=smneg[:, 4 * j + t:4 * j + t + 1],
                                     accum_out=smsum[:, 4 * j + t:4 * j + t + 1]).then_inc(s.exped, 1)

        def pt_copy(H):
            for b, (o, n) in enumerate(((0, 512), (512, 512), (1024, 256))):
                act.wait_ge(s.p_t, H + 1)
                nc.scalar.copy(pt[:, o:o + n], bank[2 + b][:, 0:n]).then_inc(s.pt_done, 1)

        def vt_copy(p):
            for j in range(2):
                act.wait_ge(s.v_t, p + 1)
                nc.scalar.copy(vt[:, j], bank[5 + j][:].rearrange("p (t d) -> p t d", t=TT)).then_inc(s.vt_ok, 1)

        def yb_copy(p, j):
            act.wait_ge(s.av_ready, 2 * p + j + 1)
            dst = yb[:, 2 * p + j] if isinstance(p, int) else yb[:, bass.ds(2 * p + j, 1)].rearrange("p a n -> p (a n)")
            nc.scalar.copy(dst, bank[5 + j][:]).then_inc(s.yb_done, 1)

        def head_evac(p, j, dst, scale):
            for m in range(2):
                act.wait_ge(s.quarter, 4 * (U_HD + j) + 2 * m + 2 + 24 * p)
                nc.scalar.activation(dst[:, m], stream[m][:], ACT.Copy, scale=scale).then_inc(s.drained, 1)

        def heads(p, lag):
            next_hi(U_HD, 6, p, 0)
            if lag:
                vt_copy(p - 1)
                pt_copy(2 * (p - 1))
            next_hi(U_HD, 6, p, 1)
            head_evac(p, 1, kf, 1.0)
            if lag:
                yb_copy(p - 1, 0)
                pt_copy(2 * (p - 1) + 1)
            next_hi(U_HD, 6, p, 2)
            if lag:
                yb_copy(p - 1, 1)
            next_hi(U_HD, 6, p, 3)
            head_evac(p, 3, qf, HD ** -0.5)
            next_hi(U_HD, 6, p, 4)
            next_hi(U_HD, 6, p, 5)
            exp_of(2 * p, 0)
            exp_of(2 * p + 1, 1)
            head_evac(p, 5, vf, 1.0)

        heads(0, False)
        with act.Fori(1, 4) as p:
            heads(p, True)
        vt_copy(3)
        pt_copy(6)
        yb_copy(3, 0)
        pt_copy(7)
        yb_copy(3, 1)
        act.wait_ge(s.av_ready, 8)
        act.wait_ge(s.yb_done, 8)
        for c in range(KR):
            nc.scalar.copy(ybhi[:, c], yb[:, c]).then_inc(s.yb_hi, 1)
        with act.Fori(0, 4) as i:
            for j in range(4):
                next_hi(U_GB, 6, i, j)
            for q in range(4):
                act.wait_ge(s.quarter, 4 * (U_GB + 3) + q + 1 + 24 * i)
                nc.scalar.activation(gb[:, q], stream[q][:], ACT.Sigmoid).then_inc(s.drained, 1)
            for j in range(4, 6):
                next_hi(U_GB, 6, i, j)
        act.wait_ge(s.quarter, 4 * (U_GB + 6 * 3 + 4))
        for c in range(KD):
            act.wait_ge(s.mix_ok, c + 1)
            nc.scalar.copy(mhi[:, c], mix[:, c]).then_inc(s.mix_hi, 1)
        with act.Fori(0, 4) as i:
            for j in range(4):
                next_hi(U_WO, 4, i, j)
        for c in range(KD):
            act.wait_ge(s.feat_t, KD + c + 1)
            nc.scalar.activation(vhi[:, c], aux[c % 4][:], ACT.Copy, scale=par[:, PR_GMLP + c:PR_GMLP + c + 1]).then_inc(s.feat_hi, 1)
        for t in range(TT):
            act.wait_ge(s.drained, B_ML)
            if t:
                act.wait_ge(s.ss2_ok, t)
            nc.scalar.activation(junk2[:], h[:, t], ACT.Square, accum_out=ss2[:, t:t + 1]).then_inc(s.ss2_ok, 1)

        def mlp(g, last):
            for b in range(2):
                for j in range(4):
                    next_hi(U_ML, 16, g, 4 * b + j)
                for q in range(4):
                    act.wait_ge(s.quarter, 4 * (U_ML + 4 * b + 3) + q + 1 + 64 * g)
                    nc.scalar.activation(relu_h[:, q], stream[q][:], ACT.Relu).then_inc(s.drained, 1)
                for q in range(4):
                    act.wait_ge(s.mlp_sq, 8 * g + 4 * b + q + 1)
                    nc.scalar.copy(hidhi[:, 4 * b + q], sq_h[:, q]).then_inc(s.mlp_hi, 1)
            for j in range(8, 16):
                if not (last and j == 15):
                    next_hi(U_ML, 16, g, j)

        with act.Fori(0, MLP_GROUPS - 1) as g:
            mlp(g, False)
        mlp(MLP_GROUPS - 1, True)
        for t in range(TT):
            act.wait_ge(s.drained, B_ML + 24 * MLP_GROUPS - 3 + t)
            nc.scalar.activation(finjunk[:], h[:, t], ACT.Square, accum_out=ss3[:, t:t + 1]).then_inc(s.fin_ss, 1)
            act.wait_ge(s.fin_ss, t + 1)
            nc.scalar.activation(ss3[:, t:t + 1], ss3[:, t:t + 1], ACT.Sqrt, bias=eps, scale=1.0 / D).then_inc(s.fin_rs, 1)
        for t in range(TT):
            act.wait_ge(s.fin_ok, t + 1)
            act.dma_start(out_t[:, t], h[:, t]).then_inc(s.out_st, 16)
        act.wait_ge(s.out_st, 16 * TT)

    @block.vector
    def _(dve):
        V = nc.vector

        def lo(n, slot, width=2048):
            dve.wait_ge(s.hi_ready, n + 1)
            V.tensor_tensor(wlo[slot][:, 0:width], raw[slot][:, 0:width], whi[slot][:, 0:width].bitcast(F32),
                            ALU.subtract).then_inc(s.lo_ready, 1)

        def next_lo(base, per, i, j):
            b = base + j + 1
            lo(b + per * i, b % 2)

        for t in range(TT):
            dve.wait_ge(s.rs_ready, t + 1)
            V.reciprocal(rs1[:, t:t + 1], ss1[:, t:t + 1]).then_inc(s.x_ready, 1)
            dve.wait_ge(s.x_ready, t + 1)
            V.tensor_scalar(xt[:, t], xt[:, t], rs1[:, t:t + 1], None, ALU.mult).then_inc(s.xs_ready, 1)
        lo(0, 0, KD * IKW)
        dve.wait_ge(s.par_ok, 1)
        la = par[:, PR_LAM:PR_LAM + 8]
        n_lam = [0]

        def lam_op(ins):
            n_lam[0] += 1
            ins.then_inc(s.lam_step, 1)
            dve.wait_ge(s.lam_step, n_lam[0])
        lam_op(V.tensor_scalar(sp_t[:, 0], la, -1.0, None, ALU.mult))
        lam_op(V.tensor_tensor(sp_t[:, 0], sp_t[:, 0], la, ALU.max))
        for c in range(KD):
            dve.wait_ge(s.feat_hi, c + 1)
            V.scalar_tensor_tensor(out=ulo[:, c], in0=aux[c % 4][:], scalar=par[:, PR_GMIX + c:PR_GMIX + c + 1],
                                   in1=uhi[:, c].bitcast(F32), op0=ALU.mult, op1=ALU.subtract).then_inc(s.feat_lo, 1)
        lo(1, 1)
        n_lam[0] += 1
        dve.wait_ge(s.lam_step, 3)
        lam_op(V.tensor_scalar(sp_t[:, 2], sp_t[:, 1], 2.0, None, ALU.add))
        lam_op(V.reciprocal(sp_t[:, 3], sp_t[:, 2]))
        lam_op(V.tensor_tensor(sp_t[:, 1], sp_t[:, 1], sp_t[:, 3], ALU.mult))
        lam_op(V.tensor_tensor(sp_t[:, 2], sp_t[:, 1], sp_t[:, 1], ALU.mult))
        lam_op(V.tensor_scalar(sp_t[:, 3], sp_t[:, 2], 1.0 / 15, 1.0 / 13, ALU.mult, ALU.add))
        for k in (11, 9, 7, 5, 3, 1):
            lam_op(V.tensor_tensor(sp_t[:, 3], sp_t[:, 3], sp_t[:, 2], ALU.mult))
            lam_op(V.tensor_scalar(sp_t[:, 3], sp_t[:, 3], 1.0 / k, None, ALU.add))
        lam_op(V.tensor_tensor(sp_t[:, 3], sp_t[:, 3], sp_t[:, 1], ALU.mult))
        lam_op(V.tensor_scalar(sp_t[:, 4], la, -1.0, 0.0, ALU.mult, ALU.max))
        lam_op(V.scalar_tensor_tensor(out=sp_t[:, 4], in0=sp_t[:, 3], scalar=2.0, in1=sp_t[:, 4],
                                      op0=ALU.mult, op1=ALU.add))
        lam_op(V.tensor_scalar(sp8, sp_t[:, 4], LRU_C, None, ALU.mult))
        lam_op(V.tensor_scalar(nsp8, sp_t[:, 4], -LRU_C, None, ALU.mult))

        dve.sem_inc(s.acc_done, 4)
        dve.wait_ge(s.mask_ok, 7)
        dve.wait_ge(s.iw_ok, 1)

        def acc_step(i, st):
            t = 1 + st % 3
            o, n = CHUNK_O[t] - P, CHUNK_W[t]
            for hh in range(2):
                b = 2 * (st % 2) + hh
                col = bass.ds(8 * i + 2 * (st // 3) + hh, 1)
                dve.wait_ge(s.acc_done, 24 * i + 2 * st + hh + 4)
                dve.wait_ge(s.relu_done, 24 * i + 2 * st + hh + 5)
                V.scalar_tensor_tensor(out=score[:, o:o + n], in0=rbuf[:, b, 0:n], scalar=iwq[:, t - 1, col],
                                       in1=score[:, o:o + n], op0=ALU.mult, op1=ALU.add).then_inc(s.acc_done, 1)

        with dve.Fori(0, 2) as i:
            for j in range(8):
                next_lo(U_IQRX, 8, i, j)
                if j >= 4:
                    for q in range(3):
                        acc_step(i, 3 * (j - 4) + q)
        step = [0]

        def tk(ins):
            step[0] += 1
            ins.then_inc(s.topk_step, 1)
        dve.wait_ge(s.acc_done, 52)
        tk(V.tensor_copy(work[:], score[:]))
        for r in range(TOPK // 8):
            if r % 2 == 0:
                n = U_RG + r // 2 + 1
                lo(n, n % 2)
            for t in range(1, TT):
                o, n = CHUNK_O[t] - P, CHUNK_W[t]
                dve.wait_ge(s.topk_step, step[0])
                tk(V.max(top8, work[:, o:o + n]))
                dve.wait_ge(s.topk_step, step[0])
                tk(V.match_replace(work[:, o:o + n], top8, work[:, o:o + n], NEG))
        for t in range(1, TT):
            o, n = CHUNK_O[t] - P, CHUNK_W[t]
            dve.wait_ge(s.topk_step, step[0])
            tk(V.tensor_tensor(work[:, o:o + n], score[:, o:o + n], work[:, o:o + n], ALU.is_gt))
            dve.wait_ge(s.topk_step, step[0])
            tk(V.tensor_scalar(work[:, o:o + n], work[:, o:o + n], -1.0, -NEG, ALU.add, ALU.mult))
            dve.wait_ge(s.topk_step, step[0])
            V.scalar_tensor_tensor(out=abias[:, o + P:o + P + n], in0=dist[:, 0:n], scalar=-float(P * t),
                                   in1=work[:, o:o + n], op0=ALU.add, op1=ALU.add).then_inc(s.sel_ok, 1)

        xc, rr, ii, aa, th = (lru[n] for n in ("xc", "rr", "ii", "aa", "th"))

        def one(t, i, j, a=0, b=S):
            return t[:, bass.ds(2 * i + j, 1), a:b].rearrange("p a n -> p (a n)")

        with dve.Fori(0, 4) as i:
            next_lo(U_GA, 4, i, 0)
            for j in range(2):
                V.tensor_scalar(xc[:, j], one(rx, i, j, PAD - 3, RXW - 3), par[:, bass.ds(PR_CW + 2 * i + j, 1)],
                                par[:, bass.ds(PR_CB + 2 * i + j, 1)], ALU.mult, ALU.add).then_inc(s.lru_v, 1)
            for k in range(1, 4):
                for j in range(2):
                    dve.wait_ge(s.lru_v, lru_dve(i, f"conv{k - 1}", j))
                    V.scalar_tensor_tensor(out=xc[:, j], in0=one(rx, i, j, PAD - 3 + k, RXW - 3 + k),
                                           scalar=par[:, bass.ds(PR_CW + 8 * k + 2 * i + j, 1)], in1=xc[:, j],
                                           op0=ALU.mult, op1=ALU.add).then_inc(s.lru_v, 1)
            next_lo(U_GA, 4, i, 1)
            for j in range(2):
                dve.wait_ge(s.lru_a, lru_act(i, "th", j))
                V.tensor_tensor(rr[:, j], aa[:, j], aa[:, j], ALU.mult).then_inc(s.lru_v, 1)
            for j in range(2):
                dve.wait_ge(s.lru_v, lru_dve(i, "asq", j))
                V.scalar_tensor_tensor(out=th[:, j], in0=rr[:, j], scalar=1.0, in1=th[:, j],
                                       op0=ALU.add, op1=ALU.mult).then_inc(s.lru_v, 1)
            next_lo(U_GA, 4, i, 2)
            for j in range(2):
                V.tensor_tensor(ii[:, j], ii[:, j], xc[:, j], ALU.mult).then_inc(s.lru_v, 1)
            for j in range(2):
                dve.wait_ge(s.lru_a, lru_act(i, "mult", j))
                dve.wait_ge(s.lru_v, lru_dve(i, "gated", j))
                V.tensor_tensor(ii[:, j], ii[:, j], rr[:, j], ALU.mult).then_inc(s.lru_v, 1)
            for j in range(2):
                dve.wait_ge(s.lru_v, lru_dve(i, "u", j))
                V.tensor_tensor_scan(th[:, j], aa[:, j], ii[:, j], 0.0, ALU.mult, ALU.add).then_inc(s.lru_v, 1)
            for j in range(2):
                dve.wait_ge(s.lru_v, lru_dve(i, "scan", j))
                V.tensor_tensor(xc[:, j], th[:, j], one(rg, i, j), ALU.mult).then_inc(s.lru_v, 1)
            for j in range(2):
                dve.wait_ge(s.lru_a, lru_act(i, "hi", j))
                V.tensor_tensor(one(yalo, i, j), xc[:, j], one(yahi, i, j).bitcast(F32), ALU.subtract).then_inc(s.lru_v, 1)
            dve.wait_ge(s.lru_v, lru_dve(i, "lo", 1))
            next_lo(U_GA, 4, i, 3)

        with dve.Fori(0, 4) as i:
            next_lo(U_WR, 2, i, 0)
            next_lo(U_WR, 2, i, 1)
            for q in range(4):
                m = mix[:, bass.ds(4 * i + q, 1)].rearrange("p a n -> p (a n)")
                dve.wait_ge(s.quarter, 4 * (U_WR + 1) + q + 1 + 8 * i)
                V.tensor_tensor(m, stream[q][:], m, ALU.mult).then_inc(s.drained, 1)

        place = [(3, 384), (4, 0), (3, 0), (2, 0)]

        def soft(H, j):
            dve.wait_ge(s.scores_ready, H + 1)
            for t in range(TT):
                b, c = place[t]
                o, n = CHUNK_O[t], CHUNK_W[t]
                V.scalar_tensor_tensor(out=sm[:, j, o:o + n], in0=abias[:, o:o + n],
                                       scalar=slopes[:, bass.ds(H, 1)], in1=bank[b + 3 * j][:, c:c + n],
                                       op0=ALU.mult, op1=ALU.add).then_inc(s.biased, 1)
            for t in range(TT):
                o, n = CHUNK_O[t], CHUNK_W[t]
                dve.wait_ge(s.biased, 4 * H + t + 1)
                V.tensor_reduce(smneg[:, 4 * j + t:4 * j + t + 1], sm[:, j, o:o + n], AX.X, ALU.max,
                                negate=True).then_inc(s.negmax, 1)

        def quotient(H, j):
            dve.wait_ge(s.exped, 4 * H + 4)
            V.reciprocal(sminv[:, 4 * j:4 * j + 4], smsum[:, 4 * j:4 * j + 4]).then_inc(s.recip, 1)
            dve.wait_ge(s.recip, H + 1)
            for t in range(TT):
                o, n = CHUNK_O[t], CHUNK_W[t]
                V.tensor_scalar(sm[:, j, o:o + n], sm[:, j, o:o + n], sminv[:, 4 * j + t:4 * j + t + 1], None,
                                ALU.mult).then_inc(s.normed, 1)

        with dve.Fori(0, 4) as p:
            for j in range(5):
                next_lo(U_HD, 6, p, j)
            soft(2 * p, 0)
            soft(2 * p + 1, 1)
            next_lo(U_HD, 6, p, 5)
            quotient(2 * p, 0)
            quotient(2 * p + 1, 1)
        dve.wait_ge(s.av_ready, 8)
        for c in range(KR):
            dve.wait_ge(s.yb_hi, c + 1)
            V.tensor_tensor(yblo[:, c], yb[:, c], ybhi[:, c].bitcast(F32), ALU.subtract).then_inc(s.yb_lo, 1)
        with dve.Fori(0, 4) as i:
            for j in range(6):
                next_lo(U_GB, 6, i, j)
            for q in range(4):
                m = mix[:, bass.ds(4 * i + q, 1)].rearrange("p a n -> p (a n)")
                if q >= 2:
                    dve.wait_ge(s.mix_ok, 4 * i + q - 1)
                dve.wait_ge(s.quarter, 4 * (U_GB + 5) + q + 1 + 24 * i)
                V.tensor_tensor(ga_tmp[:, q % 2], stream[q][:], gb[:, q], ALU.mult).then_inc(s.drained, 1)
                dve.wait_ge(s.drained, B_GB + 4 + q + 1 + 8 * i)
                V.tensor_tensor(m, m, ga_tmp[:, q % 2], ALU.add).then_inc(s.mix_ok, 1)
        for c in range(KD):
            dve.wait_ge(s.mix_hi, c + 1)
            V.tensor_tensor(mlo[:, c], mix[:, c], mhi[:, c].bitcast(F32), ALU.subtract).then_inc(s.mix_lo, 1)
        dve.wait_ge(s.h_in, 16)
        with dve.Fori(0, 4) as i:
            for j in range(4):
                next_lo(U_WO, 4, i, j)
            for t in range(TT):
                v = h[:, t, bass.ds(512 * i, 512)]
                dve.wait_ge(s.quarter, 4 * (U_WO + 3) + t + 1 + 16 * i)
                V.tensor_tensor(v, stream[t][:], v, ALU.add).then_inc(s.drained, 1)
        for c in range(KD):
            dve.wait_ge(s.feat_hi, KD + c + 1)
            V.scalar_tensor_tensor(out=vlo[:, c], in0=aux[c % 4][:], scalar=par[:, PR_GMLP + c:PR_GMLP + c + 1],
                                   in1=vhi[:, c].bitcast(F32), op0=ALU.mult, op1=ALU.subtract).then_inc(s.feat_lo, 1)
        dve.wait_ge(s.ss2_ok, TT)
        V.tensor_scalar(ss2, ss2, 1.0 / D, EPS, ALU.mult, ALU.add).then_inc(s.rs2_ok, 1)
        dve.wait_ge(s.rs2_ok, 1)
        V.reciprocal(rs2, ss2).then_inc(s.rs2_ok, 1)
        dve.wait_ge(s.rs2_ok, 2)

        def mlp(g, last):
            for b in range(2):
                for j in range(4):
                    next_lo(U_ML, 16, g, 4 * b + j)
                for q in range(4):
                    dve.wait_ge(s.drained, B_ML + 4 * b + q + 1 + 24 * g)
                    V.tensor_tensor(sq_h[:, q], relu_h[:, q], relu_h[:, q], ALU.mult).then_inc(s.mlp_sq, 1)
                for q in range(4):
                    dve.wait_ge(s.mlp_hi, 8 * g + 4 * b + q + 1)
                    V.tensor_tensor(hidlo[:, 4 * b + q], sq_h[:, q], hidhi[:, 4 * b + q].bitcast(F32),
                                    ALU.subtract).then_inc(s.mlp_lo, 1)
            for c in range(4):
                for kh in range(2):
                    j = 8 + 2 * c + kh
                    if not (last and j == 15):
                        next_lo(U_ML, 16, g, j)
                for t in range(TT):
                    v = h[:, t, 512 * c:512 * c + 512]
                    dve.wait_ge(s.quarter, 4 * (U_ML + 9 + 2 * c) + t + 1 + 64 * g)
                    V.scalar_tensor_tensor(out=v, in0=stream[t][:], scalar=rs2[:, t:t + 1], in1=v,
                                           op0=ALU.mult, op1=ALU.add).then_inc(s.drained, 1)

        with dve.Fori(0, MLP_GROUPS - 1) as g:
            mlp(g, False)
        mlp(MLP_GROUPS - 1, True)
        dve.wait_ge(s.g_in, 16)
        for t in range(TT):
            dve.wait_ge(s.fin_rs, t + 1)
            V.reciprocal(rs3[:, t:t + 1], ss3[:, t:t + 1]).then_inc(s.x_ready, 1)
            dve.wait_ge(s.x_ready, TT + t + 1)
            V.scalar_tensor_tensor(out=h[:, t], in0=h[:, t], scalar=rs3[:, t:t + 1], in1=gfin[:],
                                   op0=ALU.mult, op1=ALU.mult).then_inc(s.fin_ok, 1)

    @block.tensor
    def _(pe):
        T = nc.tensor
        PE_ONLY = [pe.engine]

        def loop(a, b):
            return nc.Fori(a, b, engines=PE_ONLY, hint_back_edge=True)

        def products(dst, pairs, first, last):
            n = len(pairs)
            for k, (ah, al, bh, bl) in enumerate(pairs):
                T.matmul(dst, ah, bh, start=first and k == 0, stop=False)
                T.matmul(dst, ah, bl, start=False, stop=False)
                ins = T.matmul(dst, al, bh, start=False, stop=last and k == n - 1)
            return ins

        def feature_unit(n, slot, hi_t, lo_t, k0, first, last, free):
            pe.wait_ge(s.lo_ready, n + 1)
            wh, wl = four(whi[slot]), four(wlo[slot])
            for m in range(4):
                if first and free is not None:
                    pe.wait_ge(s.drained, free + m + 1)
                c = slice(P * m, P * m + P)
                products(stream[m][:], [(wh[:, k, c], wl[:, k, c], hi_t[:, k0 + k, 0:S], lo_t[:, k0 + k, 0:S])
                                        for k in range(4)], first, last).then_inc(s.quarter, 1)
                yield m

        def token_unit(n, slot, hi_t, lo_t, k0, first, last, free):
            pe.wait_ge(s.lo_ready, n + 1)
            wh, wl = four(whi[slot]), four(wlo[slot])
            for t in range(TT):
                if first:
                    pe.wait_ge(s.drained, free + t + 1)
                c = slice(P * t, P * t + P)
                products(stream[t][:], [(hi_t[:, k0 + k, c], lo_t[:, k0 + k, c], wh[:, k], wl[:, k])
                                        for k in range(4)], first, last).then_inc(s.quarter, 1)

        def feature_block(base, i, per, off, units, hi_t, lo_t, free, k0=0):
            for j in range(units):
                for _ in feature_unit(base + off + j + per * i, (base + off + j) % 2, hi_t, lo_t, k0 + 4 * j,
                                      j == 0, j == units - 1, free):
                    pass

        def turn(src, count):
            for c in range(KD):
                if c >= 4:
                    pe.wait_ge(s.feat_lo, count + c - 3)
                for t in range(TT):
                    ins = T.transpose(aux[c % 4][:, P * t:P * t + P], src[:, t, P * c:P * c + P], ident[:])
                ins.then_inc(s.feat_t, 1)

        pe.wait_ge(s.ident_ok, 1)
        pe.wait_ge(s.par_in, 16 * 7)
        T.transpose(bank[3][:, 0:PR_ROWS], par_rows[:], ident[0:PR_ROWS, 0:PR_ROWS]).then_inc(s.par_t, 1)
        pe.wait_ge(s.xs_ready, TT)
        turn(xt, 0)
        pe.wait_ge(s.lo_ready, 1)
        pe.wait_ge(s.feat_lo, KD)
        wh = whi[0][:, 0:KD * IKW].rearrange("p (k n) -> p k n", k=KD)
        wl = wlo[0][:, 0:KD * IKW].rearrange("p (k n) -> p k n", k=KD)
        for q in range(4):
            products(stream[0][0:IKW, :], [(wh[:, k], wl[:, k], uhi[:, k], ulo[:, k]) for k in range(4 * q, 4 * q + 4)],
                     q == 0, q == 3).then_inc(s.quarter, 1)
        pe.wait_ge(s.drained, 1)
        for t in range(1, TT):
            ins = T.transpose(aux[0][:, IKW * (t - 1):IKW * t], ikw[0:IKW, P * t:P * t + P], ident[0:IKW, 0:IKW])
        ins.then_inc(s.iwt, 1)

        pe.wait_ge(s.ikd_in, 16)
        pe.wait_ge(s.iw_ok, 1)

        def idx_step(i, st):
            j, t = st // 3, 1 + st % 3
            for hh in range(2):
                b = 2 * (st % 2) + hh
                r = slice(IDX_DIM * hh, IDX_DIM * hh + IDX_DIM)
                pe.wait_ge(s.relu_done, 24 * i + 2 * st + hh + 1)
                keys = ikw if hh == 0 else ikd
                T.matmul(aux[b][:, 0:CHUNK_W[t]], iq[r, j, P * t:P * t + P], keys[r, 0:CHUNK_W[t]],
                         start=True, stop=True).then_inc(s.idx_mm, 1)

        with loop(0, 2) as i:
            n = U_IQRX + 8 * i
            pe.wait_ge(s.drained, B_IQRX + 8 * i)
            feature_block(U_IQRX, i, 8, 0, 4, uhi, ulo, None)
            for j in range(4, 8):
                for q in feature_unit(n + j, (U_IQRX + j) % 2, uhi, ulo, 4 * (j - 4), j == 4, j == 7,
                                      B_IQRX + 8 * i):
                    if q < 3:
                        if j == 4 and q == 0:
                            pe.wait_ge(s.drained, B_IQRX + 4 + 8 * i)
                        idx_step(i, 3 * (j - 4) + q)
        with loop(0, 2) as i:
            feature_block(U_RG, i, 4, 0, 4, uhi, ulo, B_RG - 4 + 4 * i)
        with loop(0, 4) as i:
            for j in range(4):
                for _ in feature_unit(U_GA + j + 4 * i, (U_GA + j) % 2, uhi, ulo, 4 * j, j == 0, j == 3,
                                      B_GA - 4 + 4 * i):
                    pass
                if j == 0:
                    pe.wait_ge(s.bd_in, 128 * i + 128)
                    for jj in range(2):
                        pe.wait_ge(s.lru_v, lru_dve(i, "conv3", jj))
                        T.matmul(aux[2 * jj][:], bd[:, jj, 0], lru["xc"][:, jj], start=True, stop=True)
                        T.matmul(aux[2 * jj + 1][:], bd[:, jj, 1], lru["xc"][:, jj], start=True,
                                 stop=True).then_inc(s.lru_mm, 1)
        pe.wait_ge(s.lru_v, lru_dve(3, "lo", 1))
        with loop(0, 4) as i:
            feature_block(U_WR, i, 2, 0, 2, yahi, yalo, B_WR - 4 + 4 * i)

        def pair_unit(n, slot, half, free):
            pe.wait_ge(s.lo_ready, n + 1)
            wh, wl = eight(whi[slot]), eight(wlo[slot])
            for m in range(2):
                if half == 0:
                    pe.wait_ge(s.drained, free + m + 1)
                c = slice(P * m, P * m + P)
                for k0 in (0, 4):
                    products(stream[m][:], [(wh[:, k, c], wl[:, k, c], uhi[:, 8 * half + k], ulo[:, 8 * half + k])
                                            for k in range(k0, k0 + 4)],
                             half == 0 and k0 == 0, half == 1 and k0 == 4).then_inc(s.quarter, 1)

        place = [(3, 384), (4, 0), (3, 0), (2, 0)]

        def head_scores(p):
            pe.wait_ge(s.drained, B_HD + 4 + 6 * p)
            for j in range(2):
                for t in (3, 2, 0, 1):
                    b, c = place[t]
                    n = CHUNK_W[t]
                    ins = T.matmul(bank[b + 3 * j][:, c:c + n], qf[:, j, P * t:P * t + P], kf[:, j, 0:n],
                                   start=True, stop=True)
                ins.then_inc(s.scores_ready, 1)

        def turn_v(p):
            pe.wait_ge(s.drained, B_HD + 6 + 6 * p)
            for j in range(2):
                for t in range(TT):
                    ins = T.transpose(bank[5 + j][:, P * t:P * t + P], vf[:, j, P * t:P * t + P], ident[:])
            ins.then_inc(s.v_t, 1)

        def turn_p(H, j):
            pe.wait_ge(s.normed, 4 * H + 4)
            if j == 1:
                pe.wait_ge(s.pt_done, 3 * H)
            for kc in range(TT):
                b, c = [(2, 0), (3, 0), (4, 0), (3, 384)][kc]
                for t in range(kc, TT):
                    o = CHUNK_O[t] + P * kc
                    ins = T.transpose(bank[b][:, c + P * (t - kc):c + P * (t - kc) + P], sm[:, j, o:o + P], ident[:])
            ins.then_inc(s.p_t, 1)

        def values(H, j, vt_count):
            pe.wait_ge(s.pt_done, 3 * H + 3)
            pe.wait_ge(s.vt_ok, vt_count)
            for kc in range(TT):
                o = [0, 512, 1024, 896][kc]
                n = S - P * kc
                ins = T.matmul(bank[5 + j][:, P * kc:S], vt[:, j, kc], pt[:, o:o + n], start=kc == 0, stop=kc == 3)
            ins.then_inc(s.av_ready, 1)

        def heads(p, lag):
            n = U_HD + 6 * p
            d = B_HD + 6 * p
            pair_unit(n, U_HD % 2, 0, d - 2)
            if lag:
                turn_v(p - 1)
                turn_p(2 * (p - 1), 0)
            pair_unit(n + 1, (U_HD + 1) % 2, 1, 0)
            if lag:
                values(2 * (p - 1), 0, 2 * (p - 1) + 2)
                turn_p(2 * (p - 1) + 1, 1)
            pair_unit(n + 2, U_HD % 2, 0, d)
            if lag:
                values(2 * (p - 1) + 1, 1, 2 * (p - 1) + 2)
            pair_unit(n + 3, (U_HD + 1) % 2, 1, 0)
            pair_unit(n + 4, U_HD % 2, 0, d + 2)
            if lag:
                pe.wait_ge(s.yb_done, 2 * p)
            head_scores(p)
            pair_unit(n + 5, (U_HD + 1) % 2, 1, 0)

        heads(0, False)
        with loop(1, 4) as p:
            heads(p, True)
        turn_v(3)
        turn_p(6, 0)
        values(6, 0, 8)
        turn_p(7, 1)
        values(7, 1, 8)
        with loop(0, 4) as i:
            d = B_GB + 8 * i
            feature_block(U_GB, i, 6, 0, 4, uhi, ulo, d - 4)
            pe.wait_ge(s.yb_lo, KR)
            feature_block(U_GB, i, 6, 4, 2, ybhi, yblo, d)
        pe.wait_ge(s.mix_lo, KD)
        with loop(0, 4) as i:
            for j in range(4):
                token_unit(U_WO + 4 * i + j, (U_WO + j) % 2, mhi, mlo, 4 * j, j == 0, j == 3, B_WO - 4 + 4 * i)
        pe.wait_ge(s.drained, B_ML)
        turn(h, KD)
        pe.wait_ge(s.feat_lo, 2 * KD)
        with loop(0, MLP_GROUPS) as g:
            d = B_ML + 24 * g
            for b in range(2):
                feature_block(U_ML, g, 16, 4 * b, 4, vhi, vlo, d - 4 + 4 * b)
            for c in range(4):
                for kh in range(2):
                    j = 8 + 2 * c + kh
                    pe.wait_ge(s.mlp_lo, 8 * g + 4 * kh + 4)
                    token_unit(U_ML + 16 * g + j, (U_ML + j) % 2, hidhi, hidlo, 4 * kh, kh == 0, kh == 1,
                               d + 4 + 4 * c)

    block.__exit__(None, None, None)


INPUTS = ["x", "norm_mix_g", "w_in", "conv_w", "conv_b", "w_rg_r", "b_rg_r", "w_rg_i", "b_rg_i", "lru_lambda",
          "w_branch_rnn", "w_branch_attn", "w_out", "norm_mlp_g", "w_mlp_up", "w_mlp_down", "norm_final_g"]


def kernel(**inputs):
    import concourse.bacc as bacc
    from concourse.bass_utils import run_bass_kernel_spmd

    nc = bacc.Bacc("TRN2", target_bir_lowering=False, num_devices=1)
    arrays, args = {}, []
    for name in INPUTS:
        a = np.ascontiguousarray(inputs[name])
        arrays[f"in_{name}"] = a
        args.append(nc.dram_tensor(f"in_{name}", a.shape, F32, kind="ExternalInput").ap())
    args.append(nc.dram_tensor("out", (1, S, D), F32, kind="ExternalOutput").ap())
    hybrid_block(nc, *args)
    return run_bass_kernel_spmd(nc, [arrays], core_ids=[0]).results[0]["out"]
```

```python
import numpy as np

import concourse.bass as bass
from concourse import mybir

F32 = mybir.dt.float32
F32R = mybir.dt.float32r
ACT = mybir.ActivationFunctionType
ALU = mybir.AluOpType
AX = mybir.AxisListType

P = 128
S = 512
D = 2048
RNN = D // 2
HEADS = 8
HD = 128
IDX_HEADS = 16
IDX_DIM = 64
D_FF = 4 * D
TOPK = min(256, S // 4)
LRU_C = 8.0
EPS = 1e-6
TT = S // P
KD = D // P
KR = RNN // P
PAD = 4
RXW = S + PAD

C_RX, C_RG, C_Q, C_K, C_V = 0, RNN, 2 * RNN, 3 * RNN, 4 * RNN
C_IQ = 5 * RNN
C_IK = C_IQ + IDX_HEADS * IDX_DIM
C_GA = C_IK + IDX_DIM + IDX_HEADS
C_GB = C_GA + D
IKW = IDX_DIM + IDX_HEADS

U_IQRX = 1
U_RG = U_IQRX + 16
U_GA = U_RG + 8
U_WR = U_GA + 16
U_HD = U_WR + 8
U_GB = U_HD + 24
U_WO = U_GB + 24
U_ML = U_WO + 16
MLP_GROUPS = D_FF // 1024
B_IQRX = 1
B_RG = B_IQRX + 16
B_GA = B_RG + 8
B_WR = B_GA + 16
B_HD = B_WR + 16
B_GB = B_HD + 24
B_WO = B_GB + 32
B_ML = B_WO + 16

NEG = -3.0e38
CHUNK_W = [P * (t + 1) for t in range(TT)]
CHUNK_O = [sum(CHUNK_W[:t]) for t in range(TT)]
PACKED = sum(CHUNK_W)

PR_GMLP, PR_CW, PR_CB, PR_BR, PR_BI, PR_LAM = 0, 16, 48, 56, 64, 72
PR_ROWS = 80

LRU_DVE = ["conv0", "conv1", "conv2", "conv3", "asq", "var", "gated", "u", "scan", "y", "lo"]
LRU_ACT = ["r", "i", "a", "th", "mult", "hi"]


def lru_dve(i, step, j):
    return 2 * len(LRU_DVE) * i + 2 * LRU_DVE.index(step) + j + 1


def lru_act(i, step, j):
    return 2 * len(LRU_ACT) * i + 2 * LRU_ACT.index(step) + j + 1


class Semaphores:

    def __init__(self, nc):
        self.x_in = [nc.alloc_semaphore(f"x_in{t}") for t in range(TT)]
        self.gmix_in = nc.alloc_semaphore("gmix_in")
        self.ik_hi = nc.alloc_semaphore("ik_hi")
        self.ik_lo = nc.alloc_semaphore("ik_lo")
        self.iq_hi = nc.alloc_semaphore("iq_hi")
        self.kq_hi = nc.alloc_semaphore("kq_hi")
        self.fin_g = nc.alloc_semaphore("fin_g")
        self.fin_sum = nc.alloc_semaphore("fin_sum")
        self.par_in = nc.alloc_semaphore("par_in")
        self.g_in = nc.alloc_semaphore("g_in")
        self.ikd_in = nc.alloc_semaphore("ikd_in")
        self.bd_in = nc.alloc_semaphore("bd_in")
        self.h_in = nc.alloc_semaphore("h_in")
        self.out_st = nc.alloc_semaphore("out_st")
        self.ident_ok = nc.alloc_semaphore("ident_ok")
        self.zeros_ok = nc.alloc_semaphore("zeros_ok")
        self.mask_ok = nc.alloc_semaphore("mask_ok")
        self.par_t = nc.alloc_semaphore("par_t")
        self.par_ok = nc.alloc_semaphore("par_ok")
        self.lam_step = nc.alloc_semaphore("lam_step")
        self.x_ready = nc.alloc_semaphore("x_ready")
        self.xs_ready = nc.alloc_semaphore("xs_ready")
        self.ss_ready = nc.alloc_semaphore("ss_ready")
        self.rs_ready = nc.alloc_semaphore("rs_ready")
        self.feat_t = nc.alloc_semaphore("feat_t")
        self.feat_hi = nc.alloc_semaphore("feat_hi")
        self.feat_lo = nc.alloc_semaphore("feat_lo")
        self.hi_ready = nc.alloc_semaphore("hi_ready")
        self.lo_ready = nc.alloc_semaphore("lo_ready")
        self.quarter = nc.alloc_semaphore("quarter")
        self.drained = nc.alloc_semaphore("drained")
        self.iwt = nc.alloc_semaphore("iwt")
        self.iw_ok = nc.alloc_semaphore("iw_ok")
        self.idx_mm = nc.alloc_semaphore("idx_mm")
        self.relu_done = nc.alloc_semaphore("relu_done")
        self.acc_done = nc.alloc_semaphore("acc_done")
        self.topk_step = nc.alloc_semaphore("topk_step")
        self.sel_ok = nc.alloc_semaphore("sel_ok")
        self.lru_mm = nc.alloc_semaphore("lru_mm")
        self.lru_v = nc.alloc_semaphore("lru_v")
        self.lru_a = nc.alloc_semaphore("lru_a")
        self.scores_ready = nc.alloc_semaphore("scores_ready")
        self.biased = nc.alloc_semaphore("biased")
        self.negmax = nc.alloc_semaphore("negmax")
        self.exped = nc.alloc_semaphore("exped")
        self.recip = nc.alloc_semaphore("recip")
        self.normed = nc.alloc_semaphore("normed")
        self.p_t = nc.alloc_semaphore("p_t")
        self.pt_done = nc.alloc_semaphore("pt_done")
        self.v_t = nc.alloc_semaphore("v_t")
        self.vt_ok = nc.alloc_semaphore("vt_ok")
        self.av_ready = nc.alloc_semaphore("av_ready")
        self.yb_done = nc.alloc_semaphore("yb_done")
        self.yb_hi = nc.alloc_semaphore("yb_hi")
        self.yb_lo = nc.alloc_semaphore("yb_lo")
        self.mix_ok = nc.alloc_semaphore("mix_ok")
        self.mix_hi = nc.alloc_semaphore("mix_hi")
        self.mix_lo = nc.alloc_semaphore("mix_lo")
        self.ss2_ok = nc.alloc_semaphore("ss2_ok")
        self.rs2_ok = nc.alloc_semaphore("rs2_ok")
        self.mlp_hi = nc.alloc_semaphore("mlp_hi")
        self.mlp_sq = nc.alloc_semaphore("mlp_sq")
        self.mlp_lo = nc.alloc_semaphore("mlp_lo")
        self.fin_ss = nc.alloc_semaphore("fin_ss")
        self.fin_rs = nc.alloc_semaphore("fin_rs")
        self.fin_ok = nc.alloc_semaphore("fin_ok")
        self.fin_half = nc.alloc_semaphore("fin_half")
        self.raw_in = [nc.alloc_semaphore(f"raw_in{k}") for k in range(2)]


def hybrid_block(nc, x, g_mix, w_in, conv_w, conv_b, w_r, b_r, w_i, b_i, lam, w_br, w_ba, w_out,
                 g_mlp, w_up, w_down, g_fin, out):
    KB = 1024
    BASE = (nc.sbuf_base + 63) // 64 * 64

    def at(name, kb, shape, dt):
        return nc.alloc_sbuf_tensor_at(name, shape, dt, offset=BASE + int(kb * KB))

    raw = [at(f"raw{s}", 8 * s, [P, 2048], F32) for s in range(2)]
    whi = [at(f"whi{s}", 16 + 8 * s, [P, 2048], F32R) for s in range(2)]
    wlo = [at(f"wlo{s}", 32 + 8 * s, [P, 2048], F32R) for s in range(2)]
    uhi = at("uhi", 48, [P, KD, S], F32R)
    ulo = at("ulo", 80, [P, KD, S], F32R)
    mhi = at("mhi", 48, [P, KD, S], F32R)
    mlo = at("mlo", 80, [P, KD, S], F32R)
    vhi_b = at("vhi_b", 48, [P, KD // 2, S], F32R)
    vlo_b = at("vlo_b", 64, [P, KD // 2, S], F32R)
    hidhi = at("hidhi", 80, [P, 8, S], F32R)
    hidlo = at("hidlo", 96, [P, 8, S], F32R)
    R3, R4 = 112, 144
    xt = at("xt", R3, [P, TT, D], F32)
    iqhi = at("iqhi", R3, [P, 4, S], F32R)
    iqlo = at("iqlo", R3 + 8, [P, 4, S], F32R)
    ikhi = at("ikhi", R3 + 16, [P, S], F32R)
    iklo = at("iklo", R3 + 18, [P, S], F32R)
    score = at("score", R3 + 20, [P, PACKED - P], F32)
    work = at("work", R3 + 24.5, [P, PACKED - P], F32)
    dist = at("dist", R3 + 29, [P, S], F32)
    mix = at("mix", R3, [P, KD, S], F32)
    vhi_a = at("vhi_a", R3, [P, KD // 2, S], F32R)
    vlo_a = at("vlo_a", R3 + 16, [P, KD // 2, S], F32R)

    junk1 = at("junk1", R4, [P, D], F32)
    gmix = at("gmix", R4 + 16, [P, D], F32)
    rbuf = at("rbuf", R4 + 33, [P, 4, S], F32)
    ikw = at("ikw", R4 + 41, [P, S], F32)
    ikd = at("ikd", R4 + 43, [P, S], F32)
    rx = at("rx", R4, [P, KR, RXW], F32)
    yahi = at("yahi", R4, [P, KR, RXW], F32R)
    rg = at("rg", R4 + 16.125, [P, KR, S], F32)
    yalo = at("yalo", R4 + 16.125, [P, KR, S], F32R)
    lru = {n: at(f"lru_{n}", R4 + 32.125 + 4 * k, [P, 2, S], F32)
           for k, n in enumerate(["xc", "rr", "ii", "aa", "th"])}
    yb = at("yb", R4, [P, KR, S], F32)
    khi = at("khi", R4 + 16, [P, 2, S], F32R)
    klo = at("klo", R4 + 20, [P, 2, S], F32R)
    qhi = at("qhi", R4 + 24, [P, 2, S], F32R)
    qlo = at("qlo", R4 + 28, [P, 2, S], F32R)
    vf = at("vf", R4 + 32, [P, 2, S], F32)
    vt = at("vt", R4 + 36, [P, 2, TT, HD], F32)
    sm = at("sm", R4 + 40, [P, 2, PACKED], F32)
    pt = at("pt", R4 + 50, [P, PACKED], F32)
    ybhi = at("ybhi", R4 + 16, [P, KR, S], F32R)
    yblo = at("yblo", R4 + 32, [P, KR, S], F32R)
    gb = at("gb", R4 + 48, [P, 4, S], F32)
    h = at("h", R4, [P, TT, D], F32)
    relu_h = at("relu_h", R4 + 32, [P, 4, S], F32)
    sq_h = at("sq_h", R4 + 40, [P, 4, S], F32)
    junk2 = at("junk2", R4 + 48, [P, D], F32)
    finjunk = at("finjunk", R4 + 56, [P, S], F32)
    gfin = at("gfin", R4 + 48, [P, D], F32)
    ga_tmp = at("ga_tmp", R4 + 56, [P, 2, S], F32)

    top = 204.0
    ident = at("ident", top, [P, P], F32)
    par = at("par", top + 0.5, [P, PR_ROWS], F32)
    par_rows = at("par_rows", top + 0.875, [PR_ROWS, P], F32)
    bd = at("bd", R4 + 52.5, [P, 2, 2, P], F32)
    iwq = at("iwq", top + 1.375, [P, TT - 1, IDX_HEADS], F32)
    small = at("small", top + 1.5625, [P, 128], F32)
    sp_t = at("sp_t", top + 2.0625, [P, 8, 8], F32)
    slopes = at("slopes", top + 2.3125, [P, HEADS], F32)
    abias = at("abias", top - 5.0, [P, PACKED], F32)
    smneg, smsum, sminv = (small[:, 8 * k:8 * k + 8] for k in range(3))
    top8 = small[:, 24:32]
    ss1, rs1, ss2, rs2, ss3, rs3 = (small[:, 32 + 4 * k:36 + 4 * k] for k in range(6))
    sq3 = small[:, 80:96].rearrange("p (t c) -> p t c", t=TT)
    eps = small[:, 64:65]
    sp8, nsp8 = sp_t[:, 6], sp_t[:, 7]

    stream = [nc.alloc_psum_tensor(f"stream{b}", [P, S], F32) for b in range(4)]
    aux = [nc.alloc_psum_tensor(f"aux{b}", [P, S], F32) for b in range(4)]
    bank = stream + aux

    s = Semaphores(nc)
    raw_in = s.raw_in

    w_in_k = w_in[0].rearrange("(k p) n -> p k n", p=P)
    w_br_k = w_br[0].rearrange("(k p) n -> p k n", p=P)
    w_ba_k = w_ba[0].rearrange("(k p) n -> p k n", p=P)
    w_out_k = w_out[0].rearrange("(k p) n -> p k n", p=P)
    w_up_k = w_up[0].rearrange("(k p) n -> p k n", p=P)
    w_down_k = w_down[0].rearrange("(k p) n -> p k n", p=P)
    x_t = x[0].rearrange("(t p) d -> p t d", p=P)
    out_t = out[0].rearrange("(t p) d -> p t d", p=P)

    def chunks(*tensors):
        return [t[:, k, 0:S] for t in tensors for k in range(t.shape[1])]

    u_hi, u_lo = chunks(uhi), chunks(ulo)
    ya_hi, ya_lo = chunks(yahi), chunks(yalo)
    yb_hi, yb_lo = chunks(ybhi), chunks(yblo)
    m_hi, m_lo = chunks(mhi), chunks(mlo)
    v_hi, v_lo = chunks(vhi_a, vhi_b), chunks(vlo_a, vlo_b)
    hid_hi, hid_lo = chunks(hidhi), chunks(hidlo)

    def four(t):
        return t[:].rearrange("p (k n) -> p k n", k=4)

    def eight(t):
        return t[:].rearrange("p (k n) -> p k n", k=8)

    block = nc.Block()
    block.__enter__()

    @block.sync
    def _(sp):
        def load(n, slot, dst, src):
            if not isinstance(n, int) or n >= 2:
                sp.wait_ge(s.lo_ready, n - 1)
            sp.dma_start(dst, src).then_inc(raw_in[slot], 16)

        def blocks(n, cols, src, k0=0, units=4):
            for j in range(units):
                load(n + j, (U_IQRX + j) % 2, four(raw[(U_IQRX + j) % 2]),
                     src[:, k0 + 4 * j:k0 + 4 * j + 4, cols])

        sp.wait_ge(s.x_in[1], 16)
        load(0, 0, raw[0][:, 0:KD * IKW].rearrange("p (k n) -> p k n", k=KD),
             w_in_k[:, :, C_IK:C_IK + IKW])
        sp.wait_ge(s.x_in[TT - 1], 16)
        for i in range(2):
            blocks(U_IQRX + 8 * i, bass.ds(C_IQ + 512 * i, 512), w_in_k)
            blocks(U_IQRX + 8 * i + 4, bass.ds(C_RX + 512 * i, 512), w_in_k)
        with sp.Fori(0, 2) as i:
            blocks(U_RG + 4 * i, bass.ds(C_RG + 512 * i, 512), w_in_k)
        with sp.Fori(0, 4) as i:
            blocks(U_GA + 4 * i, bass.ds(C_GA + 512 * i, 512), w_in_k)
        with sp.Fori(0, 4) as i:
            blocks(U_WR + 2 * i, bass.ds(512 * i, 512), w_br_k, units=2)
        with sp.Fori(0, 4) as p:
            for j, c in enumerate((C_K, C_K, C_Q, C_Q, C_V, C_V)):
                slot = (U_HD + j) % 2
                load(U_HD + 6 * p + j, slot, eight(raw[slot]),
                     w_in_k[:, 8 * (j % 2):8 * (j % 2) + 8, bass.ds(c + 256 * p, 256)])
        with sp.Fori(0, 4) as i:
            blocks(U_GB + 6 * i, bass.ds(C_GB + 512 * i, 512), w_in_k)
            blocks(U_GB + 6 * i + 4, bass.ds(256 * (2 * i), 512), w_ba_k, units=2)
        with sp.Fori(0, 4) as i:
            blocks(U_WO + 4 * i, bass.ds(512 * i, 512), w_out_k)
        with sp.Fori(0, MLP_GROUPS) as g:
            for b in range(2):
                blocks(U_ML + 16 * g + 4 * b, bass.ds(1024 * g + 512 * b, 512), w_up_k)
            for c in range(4):
                for kh in range(2):
                    j = 8 + 2 * c + kh
                    slot = (U_ML + j) % 2
                    load(U_ML + 16 * g + j, slot, four(raw[slot]),
                         w_down_k[:, bass.ds(8 * g + 4 * kh, 4), 512 * c:512 * c + 512])
        for t in range(TT):
            sp.wait_ge(s.fin_ok, 2 * t + 2)
            sp.wait_ge(s.fin_half, t + 1)
            sp.dma_start(out_t[:, t], h[:, t]).then_inc(s.out_st, 16)
        sp.wait_ge(s.out_st, 16 * TT)

    @block.gpsimd
    def _(pool):
        pool.memset(ident[:], 0.0).then_inc(s.zeros_ok, 1)
        pool.memset(bd[:], 0.0).then_inc(s.zeros_ok, 1)
        pool.memset(eps, EPS).then_inc(s.zeros_ok, 1)
        for hh in range(HEADS):
            pool.memset(slopes[:, hh:hh + 1], 2.0 ** (-8.0 * (hh + 1) / HEADS)).then_inc(s.zeros_ok, 1)
        pool.wait_ge(s.zeros_ok, 3)
        pool.affine_select(out=ident[:], in_=ident[:], compare_op=ALU.not_equal, fill=1.0, base=0,
                           pattern=[[-1, P]], channel_multiplier=1).then_inc(s.ident_ok, 1)

        def load_bd(i):
            for j in range(2):
                for g, w in enumerate((w_r, w_i)):
                    for b in range(2):
                        pool.dma_start(bd[64 * b:64 * b + 64, j, g, 64 * b:64 * b + 64],
                                       w[0, bass.ds(4 * i + 2 * j + b, 1)].rearrange("a d e -> (a d) e")
                                       ).then_inc(s.bd_in, 16)
        load_bd(0)
        pool.wait_ge(s.feat_t, KD)
        pool.wait_ge(s.xs_ready, TT)
        pool.iota(dist[:], [[1, S]], base=0, channel_multiplier=-1,
                  allow_small_or_imprecise_dtypes=True).then_inc(s.mask_ok, 1)
        pool.memset(score[:], 0.0).then_inc(s.mask_ok, 1)
        pool.memset(rx[:, :, 0:PAD], 0.0).then_inc(s.mask_ok, 1)
        pool.wait_ge(s.mask_ok, 3)
        for t in range(1, TT):
            o = CHUNK_O[t] - P
            v = score[:, o:o + CHUNK_W[t]]
            pool.affine_select(out=v, in_=v, compare_op=ALU.is_ge, fill=NEG, base=P * t,
                               pattern=[[-1, CHUNK_W[t]]], channel_multiplier=1).then_inc(s.mask_ok, 1)
        pool.affine_select(out=abias[:, 0:P], in_=dist[:, 0:P], compare_op=ALU.is_ge, fill=NEG, base=0,
                           pattern=[[-1, P]], channel_multiplier=1).then_inc(s.mask_ok, 1)
        with pool.Fori(1, 4) as i:
            pool.wait_ge(s.lru_mm, 2 * i)
            load_bd(i)
        pool.wait_ge(s.quarter, 4 * U_WO)
        pool.wait_ge(s.mix_ok, 16)
        for i in range(4):
            if i:
                pool.wait_ge(s.drained, B_WO + 4 * i)
            pool.dma_start(h[:, :, 512 * i:512 * i + 512], x_t[:, :, 512 * i:512 * i + 512]).then_inc(s.h_in, 16)
        pool.wait_ge(s.ss2_ok, TT)
        pool.dma_start(gfin[:], g_fin.rearrange("(a d) -> a d", a=1).broadcast_to([P, D])).then_inc(s.g_in, 16)
        pool.wait_ge(s.g_in, 16)
        for c in range(3):
            for t in range(TT):
                pool.wait_ge(s.fin_ss, TT * c + t + 1)
                v = h[:, t, 512 * c:512 * c + 512]
                pool.tensor_tensor(v, v, gfin[:, 512 * c:512 * c + 512], ALU.mult).then_inc(s.fin_g, 1)

    @block.scalar
    def _(act):
        for t in range(TT):
            act.dma_start(xt[:, t], x_t[:, t]).then_inc(s.x_in[t], 16)
            if t == 0:
                act.dma_start(gmix[:], g_mix.broadcast_to([P, D])).then_inc(s.gmix_in, 16)
        for row, src, n in ((PR_GMLP, g_mlp[0], 16), (PR_CB, conv_b[0], 8),
                            (PR_BR, b_r[0], 8), (PR_BI, b_i[0], 8), (PR_LAM, lam[0], 8)):
            act.dma_start(par_rows[row:row + n, :], src.rearrange("(c p) -> c p", p=P)).then_inc(s.par_in, 16)
        act.dma_start(par_rows[PR_CW:PR_CW + 32, :],
                      conv_w[0].rearrange("j (c p) -> (j c) p", p=P)).then_inc(s.par_in, 16)

        def hi(n, slot, landed, width=2048):
            act.wait_ge(raw_in[slot], 16 * landed)
            if not isinstance(n, int) or n >= 2:
                act.wait_ge(s.quarter, 4 * n - 4)
            nc.scalar.copy(whi[slot][:, 0:width], raw[slot][:, 0:width]).then_inc(s.hi_ready, 1)

        def next_hi(base, per, i, j):
            b = base + j + 1
            hi(b + per * i, b % 2, b // 2 + 1 + (per // 2) * i)

        act.wait_ge(s.zeros_ok, 3)
        nc.scalar.activation(small[:, 96:97], eps, ACT.Sqrt)

        def u_hi_part(t):
            for k in range(4):
                act.wait_ge(s.feat_t, 4 * t + k + 1)
                nc.scalar.copy(uhi[:, 4 * k:4 * k + 4, P * t:P * t + P],
                               aux[k][:].rearrange("p (c n) -> p c n", c=4)).then_inc(s.feat_hi, 1)

        for t in range(TT):
            act.wait_ge(s.x_in[t], 16)
            if t:
                act.wait_ge(s.ss_ready, t)
            nc.scalar.activation(junk1[:], xt[:, t], ACT.Square, accum_out=ss1[:, t:t + 1]).then_inc(s.ss_ready, 1)
            act.wait_ge(s.ss_ready, t + 1)
            nc.scalar.activation(ss1[:, t:t + 1], ss1[:, t:t + 1], ACT.Sqrt, bias=eps, scale=1.0 / D).then_inc(s.rs_ready, 1)
            if t:
                u_hi_part(t - 1)
        hi(0, 0, 1, KD * IKW)
        u_hi_part(TT - 1)
        act.wait_ge(s.par_t, 1)
        nc.scalar.copy(par[:], bank[3][:, 0:PR_ROWS]).then_inc(s.par_ok, 1)
        act.wait_ge(s.lam_step, 2)
        nc.scalar.activation(sp_t[:, 1], sp_t[:, 0], ACT.Exp, scale=-1.0).then_inc(s.lam_step, 1)
        hi(1, 1, 1)
        act.wait_ge(s.quarter, 4)
        act.wait_ge(s.feat_lo, KD)
        nc.scalar.copy(ikw[0:IKW, :], stream[0][0:IKW, :]).then_inc(s.drained, 1)
        act.wait_ge(s.drained, 1)
        act.dma_start(ikd[IDX_DIM:2 * IDX_DIM, :], ikw[0:IDX_DIM, :]).then_inc(s.ikd_in, 16)
        nc.scalar.copy(ikhi[0:IDX_DIM, :], ikw[0:IDX_DIM, :]).then_inc(s.ik_hi, 1)
        act.wait_ge(s.iwt, 1)
        nc.scalar.activation(iwq[:], aux[0][:, 0:(TT - 1) * IKW].rearrange("p (t c) -> p t c", t=TT - 1)[:, :, IDX_DIM:IKW],
                             ACT.Copy, scale=IDX_DIM ** -0.5 * IDX_HEADS ** -0.5).then_inc(s.iw_ok, 1)
        act.wait_ge(s.ikd_in, 16)
        nc.scalar.copy(ikhi[IDX_DIM:P, :], ikd[IDX_DIM:P, :]).then_inc(s.ik_hi, 1)
        act.sem_inc(s.relu_done, 4)

        def relu_step(i, st):
            t = 1 + st % 3
            for hh in range(2):
                b = 2 * (st % 2) + hh
                act.wait_ge(s.acc_done, 24 * i + 2 * st + hh + 1)
                act.wait_ge(s.idx_mm, 24 * i + 2 * st + hh + 1)
                nc.scalar.activation(rbuf[:, b, 0:CHUNK_W[t]], aux[b][:, 0:CHUNK_W[t]], ACT.Relu).then_inc(s.relu_done, 1)

        with act.Fori(0, 2) as i:
            for j in range(8):
                next_hi(U_IQRX, 8, i, j)
                for q in range(4):
                    if j == 3:
                        act.wait_ge(s.quarter, 4 * (U_IQRX + 3) + q + 1 + 32 * i)
                        nc.scalar.copy(iqhi[:, q], stream[q][:]).then_inc(s.iq_hi, 1)
                    if j == 7:
                        act.wait_ge(s.quarter, 4 * (U_IQRX + 7) + q + 1 + 32 * i)
                        nc.scalar.copy(rx[:, bass.ds(4 * i + q, 1), PAD:RXW].rearrange("p a n -> p (a n)"), stream[q][:]).then_inc(s.drained, 1)
                    if j >= 4 and q < 3:
                        relu_step(i, 3 * (j - 4) + q)
        with act.Fori(0, 2) as i:
            for j in range(4):
                next_hi(U_RG, 4, i, j)
            for q in range(4):
                act.wait_ge(s.quarter, 4 * (U_RG + 3) + q + 1 + 16 * i)
                nc.scalar.activation(rg[:, bass.ds(4 * i + q, 1)].rearrange("p a n -> p (a n)"), stream[q][:], ACT.Gelu_apprx_tanh).then_inc(s.drained, 1)
        act.wait_ge(s.lam_step, 23)
        act.wait_ge(s.sel_ok, 3)
        with act.Fori(0, 4) as i:
            next_hi(U_GA, 4, i, 0)
            next_hi(U_GA, 4, i, 1)
            for j in range(2):
                act.wait_ge(s.lru_mm, 2 * i + j + 1)
                nc.scalar.activation(lru["rr"][:, j], aux[2 * j][:], ACT.Sigmoid, bias=par[:, bass.ds(PR_BR + 2 * i + j, 1)]).then_inc(s.lru_a, 1)
            for j in range(2):
                nc.scalar.activation(lru["ii"][:, j], aux[2 * j + 1][:], ACT.Sigmoid, bias=par[:, bass.ds(PR_BI + 2 * i + j, 1)]).then_inc(s.lru_a, 1)
            for j in range(2):
                act.wait_ge(s.lru_a, lru_act(i, "r", j))
                nc.scalar.activation(lru["aa"][:, j], lru["rr"][:, j], ACT.Exp, scale=nsp8[:, bass.ds(2 * i + j, 1)]).then_inc(s.lru_a, 1)
            for j in range(2):
                nc.scalar.activation(lru["th"][:, j], lru["rr"][:, j], ACT.Tanh, scale=sp8[:, bass.ds(2 * i + j, 1)]).then_inc(s.lru_a, 1)
            next_hi(U_GA, 4, i, 2)
            for j in range(2):
                act.wait_ge(s.lru_v, lru_dve(i, "var", j))
                nc.scalar.activation(lru["rr"][:, j], lru["th"][:, j], ACT.Sqrt).then_inc(s.lru_a, 1)
            for j in range(2):
                act.wait_ge(s.lru_v, lru_dve(i, "y", j))
                nc.scalar.copy(yahi[:, bass.ds(2 * i + j, 1), 0:S].rearrange("p a n -> p (a n)"), lru["xc"][:, j]).then_inc(s.lru_a, 1)
            next_hi(U_GA, 4, i, 3)
            for q in range(4):
                act.wait_ge(s.quarter, 4 * (U_GA + 3) + q + 1 + 16 * i)
                nc.scalar.activation(mix[:, bass.ds(4 * i + q, 1)].rearrange("p a n -> p (a n)"), stream[q][:], ACT.Sigmoid).then_inc(s.drained, 1)
        with act.Fori(0, 4) as i:
            next_hi(U_WR, 2, i, 0)
            next_hi(U_WR, 2, i, 1)

        def exp_of(H, j):
            act.wait_ge(s.negmax, 4 * H + 4)
            for t in range(TT):
                o = CHUNK_O[t]
                v = sm[:, j, o:o + CHUNK_W[t]]
                nc.scalar.activation(v, v, ACT.Exp, bias=smneg[:, 4 * j + t:4 * j + t + 1],
                                     accum_out=smsum[:, 4 * j + t:4 * j + t + 1]).then_inc(s.exped, 1)

        def pt_copy(H, banks=(2, 3, 4)):
            for b, (o, n) in enumerate(((0, 512), (512, 512), (1024, 256))):
                act.wait_ge(s.p_t, H + 1)
                nc.scalar.copy(pt[:, o:o + n], bank[banks[b]][:, 0:n]).then_inc(s.pt_done, 1)

        def vt_copy(p):
            for j in range(2):
                act.wait_ge(s.v_t, p + 1)
                nc.scalar.copy(vt[:, j], bank[5 + j][:].rearrange("p (t d) -> p t d", t=TT)).then_inc(s.vt_ok, 1)

        def yb_copy(p, j):
            act.wait_ge(s.av_ready, 2 * p + j + 1)
            dst = yb[:, 2 * p + j] if isinstance(p, int) else yb[:, bass.ds(2 * p + j, 1)].rearrange("p a n -> p (a n)")
            nc.scalar.copy(dst, bank[5 + j][:]).then_inc(s.yb_done, 1)

        def head_hi(p, j, dst, scale):
            for m in range(2):
                act.wait_ge(s.quarter, 4 * (U_HD + j) + 2 * m + 2 + 24 * p)
                nc.scalar.activation(dst[:, m], stream[m][:], ACT.Copy, scale=scale).then_inc(s.kq_hi, 1)

        def heads(p, lag):
            next_hi(U_HD, 6, p, 0)
            if lag:
                vt_copy(p - 1)
                pt_copy(2 * (p - 1))
            next_hi(U_HD, 6, p, 1)
            head_hi(p, 1, khi, 1.0)
            if lag:
                yb_copy(p - 1, 0)
                pt_copy(2 * (p - 1) + 1)
            next_hi(U_HD, 6, p, 2)
            if lag:
                yb_copy(p - 1, 1)
            next_hi(U_HD, 6, p, 3)
            head_hi(p, 3, qhi, HD ** -0.5)
            next_hi(U_HD, 6, p, 4)
            next_hi(U_HD, 6, p, 5)
            exp_of(2 * p, 0)
            exp_of(2 * p + 1, 1)

        heads(0, False)
        with act.Fori(1, 4) as p:
            heads(p, True)
        def gate_b(i, first, last):
            next_hi(U_GB, 6, i, 0)
            if first:
                vt_copy(3)
                pt_copy(6, (4, 7, 6))
            next_hi(U_GB, 6, i, 1)
            if first:
                yb_copy(3, 0)
                pt_copy(7, (4, 7, 5))
            next_hi(U_GB, 6, i, 2)
            if first:
                yb_copy(3, 1)
                act.wait_ge(s.yb_done, HEADS)
                for c in range(KR):
                    nc.scalar.copy(ybhi[:, c], yb[:, c]).then_inc(s.yb_hi, 1)
            next_hi(U_GB, 6, i, 3)
            for q in range(4):
                act.wait_ge(s.quarter, 4 * (U_GB + 3) + q + 1 + 24 * i)
                nc.scalar.activation(gb[:, q], stream[q][:], ACT.Sigmoid).then_inc(s.drained, 1)
            next_hi(U_GB, 6, i, 4)
            if last:
                for c in range(KD - 4):
                    act.wait_ge(s.mix_ok, c + 1)
                    nc.scalar.copy(mhi[:, c], mix[:, c]).then_inc(s.mix_hi, 1)
            next_hi(U_GB, 6, i, 5)

        gate_b(0, True, False)
        with act.Fori(1, 3) as i:
            gate_b(i, False, False)
        gate_b(3, False, True)
        for c in range(KD - 4, KD):
            act.wait_ge(s.mix_ok, c + 1)
            nc.scalar.copy(mhi[:, c], mix[:, c]).then_inc(s.mix_hi, 1)

        def v_hi_part(c0):
            for c in range(c0, c0 + 4):
                act.wait_ge(s.feat_t, KD + c + 1)
                nc.scalar.activation(v_hi[c], aux[c % 4][:], ACT.Copy,
                                     scale=par[:, PR_GMLP + c:PR_GMLP + c + 1]).then_inc(s.feat_hi, 1)

        with act.Fori(0, 3) as i:
            for j in range(4):
                next_hi(U_WO, 4, i, j)
        next_hi(U_WO, 4, 3, 0)
        v_hi_part(0)
        next_hi(U_WO, 4, 3, 1)
        v_hi_part(4)
        next_hi(U_WO, 4, 3, 2)
        next_hi(U_WO, 4, 3, 3)
        act.wait_ge(s.quarter, 4 * U_ML)
        v_hi_part(8)

        def mlp(g, first, last):
            for b in range(2):
                for j in range(4):
                    next_hi(U_ML, 16, g, 4 * b + j)
                    if first and b == 0 and j == 0:
                        v_hi_part(12)
                    if first and b == 0 and j == 1:
                        for t in range(TT):
                            if t:
                                act.wait_ge(s.ss2_ok, t)
                            act.wait_ge(s.drained, B_ML)
                            nc.scalar.activation(junk2[:], h[:, t], ACT.Square,
                                                 accum_out=ss2[:, t:t + 1]).then_inc(s.ss2_ok, 1)
                for q in range(4):
                    act.wait_ge(s.quarter, 4 * (U_ML + 4 * b + 3) + q + 1 + 64 * g)
                    nc.scalar.activation(relu_h[:, q], stream[q][:], ACT.Relu).then_inc(s.drained, 1)
                for q in range(4):
                    act.wait_ge(s.mlp_sq, 8 * g + 4 * b + q + 1)
                    nc.scalar.copy(hidhi[:, 4 * b + q], sq_h[:, q]).then_inc(s.mlp_hi, 1)
            for c in range(4):
                for kh in range(2):
                    j = 8 + 2 * c + kh
                    if not (last and j == 15):
                        next_hi(U_ML, 16, g, j)
                if last:
                    for t in range(TT):
                        act.wait_ge(s.drained, B_ML + 24 * g + 8 + 4 * c + t + 1)
                        if c or t:
                            act.wait_ge(s.fin_ss, 4 * c + t)
                        nc.scalar.activation(finjunk[:], h[:, t, 512 * c:512 * c + 512], ACT.Square,
                                             accum_out=sq3[:, t, c:c + 1]).then_inc(s.fin_ss, 1)
                        if c == 3:
                            act.wait_ge(s.fin_sum, t + 1)
                            nc.scalar.activation(ss3[:, t:t + 1], ss3[:, t:t + 1], ACT.Sqrt, bias=eps,
                                                 scale=1.0 / D).then_inc(s.fin_rs, 1)
                            act.wait_ge(s.fin_g, 8 + t + 1)
                            act.wait_ge(s.x_ready, TT + t + 1)
                            nc.scalar.activation(h[:, t, 0:1024], h[:, t, 0:1024], ACT.Copy,
                                                 scale=rs3[:, t:t + 1]).then_inc(s.fin_half, 1)

        mlp(0, True, False)
        with act.Fori(1, MLP_GROUPS - 1) as g:
            mlp(g, False, False)
        mlp(MLP_GROUPS - 1, False, True)

    @block.vector
    def _(dve):
        V = nc.vector

        def lo(n, slot, width=2048):
            dve.wait_ge(s.hi_ready, n + 1)
            V.tensor_tensor(wlo[slot][:, 0:width], raw[slot][:, 0:width], whi[slot][:, 0:width].bitcast(F32),
                            ALU.subtract).then_inc(s.lo_ready, 1)

        def next_lo(base, per, i, j):
            b = base + j + 1
            lo(b + per * i, b % 2)

        def u_lo_part(t):
            for k in range(4):
                dve.wait_ge(s.feat_hi, 4 * t + k + 1)
                part = ulo[:, 4 * k:4 * k + 4, P * t:P * t + P]
                V.tensor_tensor(part, aux[k][:].rearrange("p (c n) -> p c n", c=4),
                                uhi[:, 4 * k:4 * k + 4, P * t:P * t + P].bitcast(F32),
                                ALU.subtract).then_inc(s.feat_lo, 1)

        for t in range(TT):
            dve.wait_ge(s.rs_ready, t + 1)
            V.reciprocal(rs1[:, t:t + 1], ss1[:, t:t + 1]).then_inc(s.x_ready, 1)
            dve.wait_ge(s.x_ready, t + 1)
            dve.wait_ge(s.gmix_in, 16)
            V.scalar_tensor_tensor(out=xt[:, t], in0=xt[:, t], scalar=rs1[:, t:t + 1], in1=gmix[:],
                                   op0=ALU.mult, op1=ALU.mult).then_inc(s.xs_ready, 1)
            if t:
                u_lo_part(t - 1)
        lo(0, 0, KD * IKW)
        u_lo_part(TT - 1)
        dve.wait_ge(s.par_ok, 1)
        la = par[:, PR_LAM:PR_LAM + 8]
        n_lam = [0]

        def lam_op(ins):
            n_lam[0] += 1
            ins.then_inc(s.lam_step, 1)
            dve.wait_ge(s.lam_step, n_lam[0])
        lam_op(V.tensor_scalar(sp_t[:, 0], la, -1.0, None, ALU.mult))
        lam_op(V.tensor_tensor(sp_t[:, 0], sp_t[:, 0], la, ALU.max))
        lo(1, 1)
        n_lam[0] += 1
        dve.wait_ge(s.lam_step, 3)
        lam_op(V.tensor_scalar(sp_t[:, 2], sp_t[:, 1], 2.0, None, ALU.add))
        lam_op(V.reciprocal(sp_t[:, 3], sp_t[:, 2]))
        lam_op(V.tensor_tensor(sp_t[:, 1], sp_t[:, 1], sp_t[:, 3], ALU.mult))
        lam_op(V.tensor_tensor(sp_t[:, 2], sp_t[:, 1], sp_t[:, 1], ALU.mult))
        lam_op(V.tensor_scalar(sp_t[:, 3], sp_t[:, 2], 1.0 / 15, 1.0 / 13, ALU.mult, ALU.add))
        for k in (11, 9, 7, 5, 3, 1):
            lam_op(V.tensor_tensor(sp_t[:, 3], sp_t[:, 3], sp_t[:, 2], ALU.mult))
            lam_op(V.tensor_scalar(sp_t[:, 3], sp_t[:, 3], 1.0 / k, None, ALU.add))
        lam_op(V.tensor_tensor(sp_t[:, 3], sp_t[:, 3], sp_t[:, 1], ALU.mult))
        lam_op(V.tensor_scalar(sp_t[:, 4], la, -1.0, 0.0, ALU.mult, ALU.max))
        lam_op(V.scalar_tensor_tensor(out=sp_t[:, 4], in0=sp_t[:, 3], scalar=2.0, in1=sp_t[:, 4],
                                      op0=ALU.mult, op1=ALU.add))
        lam_op(V.tensor_scalar(sp8, sp_t[:, 4], LRU_C, None, ALU.mult))
        lam_op(V.tensor_scalar(nsp8, sp_t[:, 4], -LRU_C, None, ALU.mult))

        for k, src in enumerate((ikw, ikd)):
            half = slice(IDX_DIM * k, IDX_DIM * k + IDX_DIM)
            dve.wait_ge(s.ik_hi, k + 1)
            V.tensor_tensor(iklo[half, :], src[half, :], ikhi[half, :].bitcast(F32),
                            ALU.subtract).then_inc(s.ik_lo, 1)
        dve.sem_inc(s.acc_done, 4)
        dve.wait_ge(s.mask_ok, 7)
        dve.wait_ge(s.iw_ok, 1)

        def acc_step(i, st):
            t = 1 + st % 3
            o, n = CHUNK_O[t] - P, CHUNK_W[t]
            for hh in range(2):
                b = 2 * (st % 2) + hh
                col = bass.ds(8 * i + 2 * (st // 3) + hh, 1)
                dve.wait_ge(s.acc_done, 24 * i + 2 * st + hh + 4)
                dve.wait_ge(s.relu_done, 24 * i + 2 * st + hh + 5)
                V.scalar_tensor_tensor(out=score[:, o:o + n], in0=rbuf[:, b, 0:n], scalar=iwq[:, t - 1, col],
                                       in1=score[:, o:o + n], op0=ALU.mult, op1=ALU.add).then_inc(s.acc_done, 1)

        with dve.Fori(0, 2) as i:
            for j in range(8):
                next_lo(U_IQRX, 8, i, j)
                if j == 3:
                    for q in range(4):
                        dve.wait_ge(s.iq_hi, 4 * i + q + 1)
                        V.tensor_tensor(iqlo[:, q], stream[q][:], iqhi[:, q].bitcast(F32),
                                        ALU.subtract).then_inc(s.drained, 1)
                if j >= 4:
                    for q in range(3):
                        acc_step(i, 3 * (j - 4) + q)
        step = [0]

        def tk(ins):
            step[0] += 1
            ins.then_inc(s.topk_step, 1)
        dve.wait_ge(s.acc_done, 52)
        tk(V.tensor_copy(work[:], score[:]))
        for r in range(TOPK // 8):
            for t in range(1, TT):
                o, n = CHUNK_O[t] - P, CHUNK_W[t]
                dve.wait_ge(s.topk_step, step[0])
                tk(V.max(top8, work[:, o:o + n]))
                dve.wait_ge(s.topk_step, step[0])
                tk(V.match_replace(work[:, o:o + n], top8, work[:, o:o + n], NEG))
            if r % 2 == 1:
                n = U_RG + r // 2 + 1
                lo(n, n % 2)
        for t in range(1, TT):
            o, n = CHUNK_O[t] - P, CHUNK_W[t]
            dve.wait_ge(s.topk_step, step[0])
            tk(V.tensor_tensor(work[:, o:o + n], score[:, o:o + n], work[:, o:o + n], ALU.is_gt))
            dve.wait_ge(s.topk_step, step[0])
            tk(V.tensor_scalar(work[:, o:o + n], work[:, o:o + n], -1.0, -NEG, ALU.add, ALU.mult))
            dve.wait_ge(s.topk_step, step[0])
            V.scalar_tensor_tensor(out=abias[:, o + P:o + P + n], in0=dist[:, 0:n], scalar=-float(P * t),
                                   in1=work[:, o:o + n], op0=ALU.add, op1=ALU.add).then_inc(s.sel_ok, 1)

        xc, rr, ii, aa, th = (lru[n] for n in ("xc", "rr", "ii", "aa", "th"))

        def one(t, i, j, a=0, b=S):
            return t[:, bass.ds(2 * i + j, 1), a:b].rearrange("p a n -> p (a n)")

        with dve.Fori(0, 4) as i:
            next_lo(U_GA, 4, i, 0)
            for j in range(2):
                V.tensor_scalar(xc[:, j], one(rx, i, j, PAD - 3, RXW - 3), par[:, bass.ds(PR_CW + 2 * i + j, 1)],
                                par[:, bass.ds(PR_CB + 2 * i + j, 1)], ALU.mult, ALU.add).then_inc(s.lru_v, 1)
            for k in range(1, 4):
                for j in range(2):
                    dve.wait_ge(s.lru_v, lru_dve(i, f"conv{k - 1}", j))
                    V.scalar_tensor_tensor(out=xc[:, j], in0=one(rx, i, j, PAD - 3 + k, RXW - 3 + k),
                                           scalar=par[:, bass.ds(PR_CW + 8 * k + 2 * i + j, 1)], in1=xc[:, j],
                                           op0=ALU.mult, op1=ALU.add).then_inc(s.lru_v, 1)
            next_lo(U_GA, 4, i, 1)
            for j in range(2):
                dve.wait_ge(s.lru_a, lru_act(i, "th", j))
                V.tensor_tensor(rr[:, j], aa[:, j], aa[:, j], ALU.mult).then_inc(s.lru_v, 1)
            for j in range(2):
                dve.wait_ge(s.lru_v, lru_dve(i, "asq", j))
                V.scalar_tensor_tensor(out=th[:, j], in0=rr[:, j], scalar=1.0, in1=th[:, j],
                                       op0=ALU.add, op1=ALU.mult).then_inc(s.lru_v, 1)
            next_lo(U_GA, 4, i, 2)
            for j in range(2):
                V.tensor_tensor(ii[:, j], ii[:, j], xc[:, j], ALU.mult).then_inc(s.lru_v, 1)
            for j in range(2):
                dve.wait_ge(s.lru_a, lru_act(i, "mult", j))
                dve.wait_ge(s.lru_v, lru_dve(i, "gated", j))
                V.tensor_tensor(ii[:, j], ii[:, j], rr[:, j], ALU.mult).then_inc(s.lru_v, 1)
            for j in range(2):
                dve.wait_ge(s.lru_v, lru_dve(i, "u", j))
                V.tensor_tensor_scan(th[:, j], aa[:, j], ii[:, j], 0.0, ALU.mult, ALU.add).then_inc(s.lru_v, 1)
            for j in range(2):
                dve.wait_ge(s.lru_v, lru_dve(i, "scan", j))
                V.tensor_tensor(xc[:, j], th[:, j], one(rg, i, j), ALU.mult).then_inc(s.lru_v, 1)
            for j in range(2):
                dve.wait_ge(s.lru_a, lru_act(i, "hi", j))
                V.tensor_tensor(one(yalo, i, j), xc[:, j], one(yahi, i, j).bitcast(F32), ALU.subtract).then_inc(s.lru_v, 1)
            dve.wait_ge(s.lru_v, lru_dve(i, "lo", 1))
            next_lo(U_GA, 4, i, 3)

        with dve.Fori(0, 4) as i:
            next_lo(U_WR, 2, i, 0)
            next_lo(U_WR, 2, i, 1)
            for q in range(4):
                m = mix[:, bass.ds(4 * i + q, 1)].rearrange("p a n -> p (a n)")
                dve.wait_ge(s.quarter, 4 * (U_WR + 1) + q + 1 + 8 * i)
                V.tensor_tensor(m, stream[q][:], m, ALU.mult).then_inc(s.drained, 1)

        place = [(3, 384), (4, 0), (3, 0), (2, 0)]

        def soft(H, j):
            dve.wait_ge(s.scores_ready, H + 1)
            for t in range(TT):
                b, c = place[t]
                o, n = CHUNK_O[t], CHUNK_W[t]
                V.scalar_tensor_tensor(out=sm[:, j, o:o + n], in0=abias[:, o:o + n],
                                       scalar=slopes[:, bass.ds(H, 1)], in1=bank[b + 3 * j][:, c:c + n],
                                       op0=ALU.mult, op1=ALU.add).then_inc(s.biased, 1)
            for t in range(TT):
                o, n = CHUNK_O[t], CHUNK_W[t]
                dve.wait_ge(s.biased, 4 * H + t + 1)
                V.tensor_reduce(smneg[:, 4 * j + t:4 * j + t + 1], sm[:, j, o:o + n], AX.X, ALU.max,
                                negate=True).then_inc(s.negmax, 1)

        def quotient(H, j):
            dve.wait_ge(s.exped, 4 * H + 4)
            V.reciprocal(sminv[:, 4 * j:4 * j + 4], smsum[:, 4 * j:4 * j + 4]).then_inc(s.recip, 1)
            dve.wait_ge(s.recip, H + 1)
            for t in range(TT):
                o, n = CHUNK_O[t], CHUNK_W[t]
                V.tensor_scalar(sm[:, j, o:o + n], sm[:, j, o:o + n], sminv[:, 4 * j + t:4 * j + t + 1], None,
                                ALU.mult).then_inc(s.normed, 1)

        def kq_lo(p, first, hi_t, lo_t, scale):
            for m in range(2):
                dve.wait_ge(s.kq_hi, first + m + 1 + 4 * p)
                V.scalar_tensor_tensor(out=lo_t[:, m], in0=stream[m][:], scalar=scale,
                                       in1=hi_t[:, m].bitcast(F32), op0=ALU.mult,
                                       op1=ALU.subtract).then_inc(s.drained, 1)

        with dve.Fori(0, 4) as p:
            next_lo(U_HD, 6, p, 0)
            next_lo(U_HD, 6, p, 1)
            kq_lo(p, 0, khi, klo, 1.0)
            next_lo(U_HD, 6, p, 2)
            next_lo(U_HD, 6, p, 3)
            kq_lo(p, 2, qhi, qlo, HD ** -0.5)
            next_lo(U_HD, 6, p, 4)
            soft(2 * p, 0)
            soft(2 * p + 1, 1)
            next_lo(U_HD, 6, p, 5)
            quotient(2 * p, 0)
            quotient(2 * p + 1, 1)
            for m in range(2):
                dve.wait_ge(s.quarter, 4 * (U_HD + 5) + 2 * m + 2 + 24 * p)
                V.tensor_copy(vf[:, m], stream[m][:]).then_inc(s.drained, 1)

        def gate_b(i, first, last):
            for j in range(3):
                next_lo(U_GB, 6, i, j)
            if first:
                dve.wait_ge(s.av_ready, HEADS)
                for c in range(KR):
                    dve.wait_ge(s.yb_hi, c + 1)
                    V.tensor_tensor(yblo[:, c], yb[:, c], ybhi[:, c].bitcast(F32), ALU.subtract).then_inc(s.yb_lo, 1)
            next_lo(U_GB, 6, i, 3)
            next_lo(U_GB, 6, i, 4)
            if last:
                for c in range(KD - 4):
                    dve.wait_ge(s.mix_hi, c + 1)
                    V.tensor_tensor(mlo[:, c], mix[:, c], mhi[:, c].bitcast(F32), ALU.subtract).then_inc(s.mix_lo, 1)
            next_lo(U_GB, 6, i, 5)
            for q in range(4):
                m = mix[:, 4 * i + q] if isinstance(i, int) else \
                    mix[:, bass.ds(4 * i + q, 1)].rearrange("p a n -> p (a n)")
                if q >= 2:
                    dve.wait_ge(s.mix_ok, 4 * i + q - 1)
                dve.wait_ge(s.quarter, 4 * (U_GB + 5) + q + 1 + 24 * i)
                V.tensor_tensor(ga_tmp[:, q % 2], stream[q][:], gb[:, q], ALU.mult).then_inc(s.drained, 1)
                dve.wait_ge(s.drained, B_GB + 4 + q + 1 + 8 * i)
                V.tensor_tensor(m, m, ga_tmp[:, q % 2], ALU.add).then_inc(s.mix_ok, 1)

        gate_b(0, True, False)
        with dve.Fori(1, 3) as i:
            gate_b(i, False, False)
        gate_b(3, False, True)
        for c in range(KD - 4, KD):
            dve.wait_ge(s.mix_hi, c + 1)
            V.tensor_tensor(mlo[:, c], mix[:, c], mhi[:, c].bitcast(F32), ALU.subtract).then_inc(s.mix_lo, 1)

        def v_lo_part(c0):
            for c in range(c0, c0 + 4):
                dve.wait_ge(s.feat_hi, KD + c + 1)
                V.scalar_tensor_tensor(out=v_lo[c], in0=aux[c % 4][:], scalar=par[:, PR_GMLP + c:PR_GMLP + c + 1],
                                       in1=v_hi[c].bitcast(F32), op0=ALU.mult, op1=ALU.subtract).then_inc(s.feat_lo, 1)

        def out_sums(i):
            dve.wait_ge(s.h_in, 16 * i + 16)
            for t in range(TT):
                v = h[:, t, bass.ds(512 * i, 512)]
                dve.wait_ge(s.quarter, 4 * (U_WO + 3) + t + 1 + 16 * i)
                V.tensor_tensor(v, stream[t][:], v, ALU.add).then_inc(s.drained, 1)

        with dve.Fori(0, 3) as i:
            for j in range(4):
                next_lo(U_WO, 4, i, j)
            out_sums(i)
        next_lo(U_WO, 4, 3, 0)
        v_lo_part(0)
        next_lo(U_WO, 4, 3, 1)
        v_lo_part(4)
        next_lo(U_WO, 4, 3, 2)
        next_lo(U_WO, 4, 3, 3)
        out_sums(3)
        v_lo_part(8)

        def mlp(g, first, last):
            for b in range(2):
                for j in range(4):
                    next_lo(U_ML, 16, g, 4 * b + j)
                    if first and b == 0 and j == 0:
                        v_lo_part(12)
                for q in range(4):
                    dve.wait_ge(s.drained, B_ML + 4 * b + q + 1 + 24 * g)
                    V.tensor_tensor(sq_h[:, q], relu_h[:, q], relu_h[:, q], ALU.mult).then_inc(s.mlp_sq, 1)
                for q in range(4):
                    dve.wait_ge(s.mlp_hi, 8 * g + 4 * b + q + 1)
                    V.tensor_tensor(hidlo[:, 4 * b + q], sq_h[:, q], hidhi[:, 4 * b + q].bitcast(F32),
                                    ALU.subtract).then_inc(s.mlp_lo, 1)
            if first:
                dve.wait_ge(s.ss2_ok, TT)
                V.tensor_scalar(ss2, ss2, 1.0 / D, EPS, ALU.mult, ALU.add).then_inc(s.rs2_ok, 1)
                dve.wait_ge(s.rs2_ok, 1)
                V.reciprocal(rs2, ss2).then_inc(s.rs2_ok, 1)
                dve.wait_ge(s.rs2_ok, 2)
            for c in range(4):
                for kh in range(2):
                    j = 8 + 2 * c + kh
                    if not (last and j == 15):
                        next_lo(U_ML, 16, g, j)
                for t in range(TT):
                    v = h[:, t, 512 * c:512 * c + 512]
                    dve.wait_ge(s.quarter, 4 * (U_ML + 9 + 2 * c) + t + 1 + 64 * g)
                    V.scalar_tensor_tensor(out=v, in0=stream[t][:], scalar=rs2[:, t:t + 1], in1=v,
                                           op0=ALU.mult, op1=ALU.add).then_inc(s.drained, 1)
                    if last and c == 3:
                        last_norm(t)

        def last_norm(t):
            dve.wait_ge(s.fin_ss, 12 + t + 1)
            V.tensor_reduce(ss3[:, t:t + 1], sq3[:, t], AX.X, ALU.add).then_inc(s.fin_sum, 1)
            dve.wait_ge(s.fin_rs, t + 1)
            V.reciprocal(rs3[:, t:t + 1], ss3[:, t:t + 1]).then_inc(s.x_ready, 1)
            dve.wait_ge(s.x_ready, TT + t + 1)
            dve.wait_ge(s.g_in, 16)
            V.scalar_tensor_tensor(out=h[:, t, 1536:D], in0=h[:, t, 1536:D], scalar=rs3[:, t:t + 1],
                                   in1=gfin[:, 1536:D], op0=ALU.mult, op1=ALU.mult).then_inc(s.fin_ok, 1)
            dve.wait_ge(s.fin_g, 8 + t + 1)
            V.tensor_scalar(h[:, t, 1024:1536], h[:, t, 1024:1536], rs3[:, t:t + 1], None,
                            ALU.mult).then_inc(s.fin_ok, 1)

        mlp(0, True, False)
        with dve.Fori(1, MLP_GROUPS - 1) as g:
            mlp(g, False, False)
        mlp(MLP_GROUPS - 1, False, True)

    @block.tensor
    def _(pe):
        T = nc.tensor
        PE_ONLY = [pe.engine]

        def loop(a, b):
            return nc.Fori(a, b, engines=PE_ONLY, hint_back_edge=True)

        def products(dst, pairs, first, last):
            n = len(pairs)
            for k, (ah, al, bh, bl) in enumerate(pairs):
                T.matmul(dst, ah, bh, start=first and k == 0, stop=False)
                T.matmul(dst, ah, bl, start=False, stop=False)
                ins = T.matmul(dst, al, bh, start=False, stop=last and k == n - 1)
            return ins

        def all_four(d):
            return [d - 4 + m + 1 for m in range(4)]

        def feature_unit(n, slot, hi_t, lo_t, k0, first, last, free):
            pe.wait_ge(s.lo_ready, n + 1)
            wh, wl = four(whi[slot]), four(wlo[slot])
            for m in range(4):
                if first and free is not None:
                    pe.wait_ge(s.drained, free[m])
                c = slice(P * m, P * m + P)
                products(stream[m][:], [(wh[:, k, c], wl[:, k, c], hi_t[k0 + k], lo_t[k0 + k])
                                        for k in range(4)], first, last).then_inc(s.quarter, 1)
                yield m

        def token_unit(n, slot, hi_t, lo_t, k0, first, last, free):
            pe.wait_ge(s.lo_ready, n + 1)
            wh, wl = four(whi[slot]), four(wlo[slot])
            for t in range(TT):
                if first:
                    pe.wait_ge(s.drained, free + t + 1)
                c = slice(P * t, P * t + P)
                products(stream[t][:], [(hi_t[k0 + k][:, c], lo_t[k0 + k][:, c], wh[:, k], wl[:, k])
                                        for k in range(4)], first, last).then_inc(s.quarter, 1)

        def feature_block(base, i, per, off, units, hi_t, lo_t, free, after=()):
            for j in range(units):
                for _ in feature_unit(base + off + j + per * i, (base + off + j) % 2, hi_t, lo_t, 4 * j,
                                      j == 0, j == units - 1, free):
                    pass
                if j < len(after):
                    after[j]()

        def turn_h(c0):
            for c in range(c0, c0 + 4):
                pe.wait_ge(s.feat_lo, KD + max(c - 3, 0))
                for t in range(TT):
                    ins = T.transpose(aux[c % 4][:, P * t:P * t + P], h[:, t, P * c:P * c + P], ident[:])
                ins.then_inc(s.feat_t, 1)

        pe.wait_ge(s.ident_ok, 1)
        for t in range(TT):
            pe.wait_ge(s.xs_ready, t + 1)
            for k in range(4):
                if t:
                    pe.wait_ge(s.feat_lo, 4 * (t - 1) + k + 1)
                for c in range(4 * k, 4 * k + 4):
                    ins = T.transpose(aux[k][:, P * (c % 4):P * (c % 4) + P], xt[:, t, P * c:P * c + P], ident[:])
                ins.then_inc(s.feat_t, 1)
        pe.wait_ge(s.par_in, 16 * 6)
        T.transpose(bank[3][:, 0:PR_ROWS], par_rows[:], ident[0:PR_ROWS, 0:PR_ROWS]).then_inc(s.par_t, 1)
        pe.wait_ge(s.lo_ready, 1)
        wh = whi[0][:, 0:KD * IKW].rearrange("p (k n) -> p k n", k=KD)
        wl = wlo[0][:, 0:KD * IKW].rearrange("p (k n) -> p k n", k=KD)
        for half in range(2):
            pe.wait_ge(s.feat_lo, 8 * half + 8)
            c = slice(256 * half, 256 * half + 256)
            for q in range(2):
                products(stream[0][0:IKW, c], [(wh[:, k], wl[:, k], u_hi[k][:, c], u_lo[k][:, c])
                                               for k in range(8 * q, 8 * q + 8)],
                         q == 0, q == 1).then_inc(s.quarter, 1)
        pe.wait_ge(s.drained, 1)
        for t in range(1, TT):
            ins = T.transpose(aux[0][:, IKW * (t - 1):IKW * t], ikw[0:IKW, P * t:P * t + P], ident[0:IKW, 0:IKW])
        ins.then_inc(s.iwt, 1)

        def idx_step(i, st):
            j, t = st // 3, 1 + st % 3
            for hh in range(2):
                b = 2 * (st % 2) + hh
                r = slice(IDX_DIM * hh, IDX_DIM * hh + IDX_DIM)
                pe.wait_ge(s.relu_done, 24 * i + 2 * st + hh + 1)
                c, n = slice(P * t, P * t + P), CHUNK_W[t]
                products(aux[b][:, 0:n], [(iqhi[r, j, c], iqlo[r, j, c], ikhi[r, 0:n], iklo[r, 0:n])],
                         True, True).then_inc(s.idx_mm, 1)

        with loop(0, 2) as i:
            n = U_IQRX + 8 * i
            pe.wait_ge(s.drained, B_IQRX + 8 * i)
            feature_block(U_IQRX, i, 8, 0, 4, u_hi, u_lo, None)
            pe.wait_ge(s.ik_lo, 2)
            pe.wait_ge(s.iw_ok, 1)
            for j in range(4, 8):
                for q in feature_unit(n + j, (U_IQRX + j) % 2, u_hi, u_lo, 4 * (j - 4), j == 4, j == 7,
                                      all_four(B_IQRX + 4 + 8 * i)):
                    if q < 3:
                        if j == 4 and q == 0:
                            pe.wait_ge(s.drained, B_IQRX + 4 + 8 * i)
                        idx_step(i, 3 * (j - 4) + q)
        with loop(0, 2) as i:
            feature_block(U_RG, i, 4, 0, 4, u_hi, u_lo, all_four(B_RG + 4 * i))
        with loop(0, 4) as i:
            def lru_gates():
                pe.wait_ge(s.bd_in, 128 * i + 128)
                for j in range(2):
                    pe.wait_ge(s.lru_v, lru_dve(i, "conv3", j))
                    T.matmul(aux[2 * j][:], bd[:, j, 0], lru["xc"][:, j], start=True, stop=True)
                    T.matmul(aux[2 * j + 1][:], bd[:, j, 1], lru["xc"][:, j], start=True,
                             stop=True).then_inc(s.lru_mm, 1)
            feature_block(U_GA, i, 4, 0, 4, u_hi, u_lo, all_four(B_GA + 4 * i), [lru_gates])
        pe.wait_ge(s.lru_v, lru_dve(1, "lo", 1))
        with loop(0, 4) as i:
            feature_block(U_WR, i, 2, 0, 2, ya_hi, ya_lo, all_four(B_WR + 4 * i),
                          [lambda: pe.wait_ge(s.lru_v, lru_dve(3, "lo", 1))])

        def pair_unit(n, slot, half, free):
            pe.wait_ge(s.lo_ready, n + 1)
            wh, wl = eight(whi[slot]), eight(wlo[slot])
            for m in range(2):
                if half == 0:
                    pe.wait_ge(s.drained, free + m + 1)
                c = slice(P * m, P * m + P)
                for k0 in (0, 4):
                    products(stream[m][:], [(wh[:, k, c], wl[:, k, c], u_hi[8 * half + k], u_lo[8 * half + k])
                                            for k in range(k0, k0 + 4)],
                             half == 0 and k0 == 0, half == 1 and k0 == 4).then_inc(s.quarter, 1)

        place = [(3, 384), (4, 0), (3, 0), (2, 0)]

        def head_scores(p):
            pe.wait_ge(s.drained, B_HD + 4 + 6 * p)
            for j in range(2):
                for t in (3, 2, 0, 1):
                    b, c = place[t]
                    n = CHUNK_W[t]
                    qs = slice(P * t, P * t + P)
                    ins = products(bank[b + 3 * j][:, c:c + n],
                                   [(qhi[:, j, qs], qlo[:, j, qs], khi[:, j, 0:n], klo[:, j, 0:n])], True, True)
                ins.then_inc(s.scores_ready, 1)

        def turn_v(p):
            pe.wait_ge(s.drained, B_HD + 6 + 6 * p)
            for j in range(2):
                for t in range(TT):
                    ins = T.transpose(bank[5 + j][:, P * t:P * t + P], vf[:, j, P * t:P * t + P], ident[:])
            ins.then_inc(s.v_t, 1)

        def turn_p(H, j, banks=(2, 3, 4)):
            pe.wait_ge(s.normed, 4 * H + 4)
            if j == 1:
                pe.wait_ge(s.pt_done, 3 * H)
            for kc in (0, 1, 3, 2):
                b, c = [(banks[0], 0), (banks[1], 0), (banks[2], 0), (banks[1], 384)][kc]
                if kc == 2 and banks[2] == 6:
                    pe.wait_ge(s.vt_ok, HEADS)
                if kc == 2 and banks[2] == 5:
                    pe.wait_ge(s.yb_done, HEADS - 1)
                for t in range(kc, TT):
                    o = CHUNK_O[t] + P * kc
                    ins = T.transpose(bank[b][:, c + P * (t - kc):c + P * (t - kc) + P], sm[:, j, o:o + P], ident[:])
            ins.then_inc(s.p_t, 1)

        def values(H, j, vt_count):
            pe.wait_ge(s.pt_done, 3 * H + 3)
            pe.wait_ge(s.vt_ok, vt_count)
            for kc in range(TT):
                o = [0, 512, 1024, 896][kc]
                n = S - P * kc
                ins = T.matmul(bank[5 + j][:, P * kc:S], vt[:, j, kc], pt[:, o:o + n], start=kc == 0, stop=kc == 3)
            ins.then_inc(s.av_ready, 1)

        def heads(p, lag):
            n = U_HD + 6 * p
            d = B_HD + 6 * p
            pair_unit(n, U_HD % 2, 0, d - 2)
            if lag:
                turn_v(p - 1)
                turn_p(2 * (p - 1), 0)
            pair_unit(n + 1, (U_HD + 1) % 2, 1, 0)
            if lag:
                values(2 * (p - 1), 0, 2 * (p - 1) + 2)
                turn_p(2 * (p - 1) + 1, 1)
            pair_unit(n + 2, U_HD % 2, 0, d)
            if lag:
                values(2 * (p - 1) + 1, 1, 2 * (p - 1) + 2)
            pair_unit(n + 3, (U_HD + 1) % 2, 1, 0)
            pair_unit(n + 4, U_HD % 2, 0, d + 2)
            if lag:
                pe.wait_ge(s.yb_done, 2 * p)
            head_scores(p)
            pair_unit(n + 5, (U_HD + 1) % 2, 1, 0)

        heads(0, False)
        with loop(1, 4) as p:
            heads(p, True)
        def gate_b(i, first):
            d = B_GB + 8 * i

            def after0():
                turn_v(3)
                turn_p(6, 0, (4, 7, 6))

            def after1():
                values(6, 0, 8)
                turn_p(7, 1, (4, 7, 5))

            def after2():
                values(7, 1, 8)
            feature_block(U_GB, i, 6, 0, 4, u_hi, u_lo, [d - 1, d, d, d] if first else all_four(d),
                          [after0, after1, after2] if first else ())
            if first:
                pe.wait_ge(s.yb_lo, KR)
            feature_block(U_GB, i, 6, 4, 2, yb_hi, yb_lo, all_four(d + 4))

        gate_b(0, True)
        with loop(1, 4) as i:
            gate_b(i, False)

        def project(i, after):
            for j in range(4):
                pe.wait_ge(s.mix_lo, 4 * j + 4)
                token_unit(U_WO + 4 * i + j, (U_WO + j) % 2, m_hi, m_lo, 4 * j, j == 0, j == 3, B_WO - 4 + 4 * i)
                if j < len(after):
                    after[j]()

        with loop(0, 3) as i:
            project(i, ())
        project(3, [lambda: turn_h(0), lambda: turn_h(4), lambda: turn_h(8)])

        def mlp(g, first):
            d = B_ML + 24 * g

            def after0():
                pe.wait_ge(s.drained, B_ML)
                turn_h(12)

            def after1():
                pe.wait_ge(s.feat_lo, KD + 12)

            def after2():
                pe.wait_ge(s.feat_lo, 2 * KD)
            for b in range(2):
                feature_block(U_ML, g, 16, 4 * b, 4, v_hi, v_lo, all_four(d + 4 * b),
                              [after0, after1, after2] if first and b == 0 else ())
            for c in range(4):
                for kh in range(2):
                    j = 8 + 2 * c + kh
                    pe.wait_ge(s.mlp_lo, 8 * g + 4 * kh + 4)
                    token_unit(U_ML + 16 * g + j, (U_ML + j) % 2, hid_hi, hid_lo, 4 * kh, kh == 0, kh == 1,
                               d + 4 + 4 * c)

        pe.wait_ge(s.feat_lo, KD + 8)
        mlp(0, True)
        with loop(1, MLP_GROUPS) as g:
            mlp(g, False)

    block.__exit__(None, None, None)


INPUTS = ["x", "norm_mix_g", "w_in", "conv_w", "conv_b", "w_rg_r", "b_rg_r", "w_rg_i", "b_rg_i", "lru_lambda",
          "w_branch_rnn", "w_branch_attn", "w_out", "norm_mlp_g", "w_mlp_up", "w_mlp_down", "norm_final_g"]


def kernel(**inputs):
    import concourse.bacc as bacc
    from concourse.bass_utils import run_bass_kernel_spmd

    nc = bacc.Bacc("TRN2", target_bir_lowering=False, num_devices=1)
    arrays, args = {}, []
    for name in INPUTS:
        a = np.ascontiguousarray(inputs[name])
        arrays[f"in_{name}"] = a
        args.append(nc.dram_tensor(f"in_{name}", a.shape, F32, kind="ExternalInput").ap())
    args.append(nc.dram_tensor("out", (1, S, D), F32, kind="ExternalOutput").ap())
    hybrid_block(nc, *args)
    return run_bass_kernel_spmd(nc, [arrays], core_ids=[0]).results[0]["out"]
```
